# Optimizing a Trainium2 kernel written in Bass

```python
import jax, jax.numpy as jnp
from jax import lax
import numpy as np

D_MODEL = 2048
BATCH = 1
SEQ = 128
DEPTH = 1
DEC_BATCH = 1
DEC_SEQ = 512
PAST_LEN = 256

GRID_W = 64
N_HEADS = 16
Q_LORA = 512
KV_LORA = 256
D_NOPE = 128
D_ROPE = 64
D_V = 128
ROPE_FREQS = D_ROPE // 4
ROPE_BASE = 10000.0
Q_BLOCK = 128
GM_WIDTH = 2048
GM_GROUPS = 8
GM_GC = GM_WIDTH // GM_GROUPS
CHUNK = 128
N_EXPERTS = 16
D_FF_EXPERT = D_MODEL // 2
EC_FACTOR = 2
IN_SPLITS = (Q_LORA, KV_LORA, D_ROPE, GM_WIDTH, GM_WIDTH, D_MODEL, D_MODEL)
IN_WIDTH = sum(IN_SPLITS)
EPS = 1e-6

kernel_name = "hybrid_mla_gmlp_ec_diffusion_step"

def rms(x, g):
    xf = x.astype(jnp.float32)
    y = xf * lax.rsqrt(jnp.mean(xf * xf, axis=-1, keepdims=True) + EPS)
    return (y * g.astype(jnp.float32)).astype(x.dtype)

def rope_angles(n):
    t = jnp.arange(n, dtype=jnp.int32)
    row = (t // GRID_W).astype(jnp.float32)
    col = (t % GRID_W).astype(jnp.float32)
    inv = 1.0 / (ROPE_BASE ** (jnp.arange(ROPE_FREQS, dtype=jnp.float32) / ROPE_FREQS))
    return jnp.stack([row[:, None] * inv, col[:, None] * inv], axis=1)

def apply_rope2d(x, ang):
    xr = x.reshape(*x.shape[:-1], 2, 2, ROPE_FREQS)
    x1, x2 = xr[..., 0, :], xr[..., 1, :]
    cos = jnp.cos(ang).astype(x.dtype)
    sin = jnp.sin(ang).astype(x.dtype)
    out = jnp.stack([x1 * cos - x2 * sin, x2 * cos + x1 * sin], axis=-2)
    return out.reshape(x.shape)

def attend(q_nope, q_rope, k_nope, k_rope, v):
    b, n, h, _ = q_nope.shape
    nb = n // Q_BLOCK
    scale = (D_NOPE + D_ROPE) ** -0.5
    qn = q_nope.reshape(b, nb, Q_BLOCK, h, D_NOPE).transpose(1, 0, 2, 3, 4)
    qr = q_rope.reshape(b, nb, Q_BLOCK, h, D_ROPE).transpose(1, 0, 2, 3, 4)

    def one_block(args):
        qn_b, qr_b = args
        s = (jnp.einsum('bqhd,bkhd->bhqk', qn_b, k_nope)
             + jnp.einsum('bqhr,bkr->bhqk', qr_b, k_rope)).astype(jnp.float32) * scale
        p = jax.nn.softmax(s, axis=-1).astype(v.dtype)
        return jnp.einsum('bhqk,bkhd->bqhd', p, v)

    o = lax.map(one_block, (qn, qr))
    return o.transpose(1, 0, 2, 3, 4).reshape(b, n, h * D_V)

def spatial_gating(gu, gv, g_sgu, w_s, b_s):
    b, n, _ = gu.shape
    v = rms(gv, g_sgu).reshape(b, n // CHUNK, CHUNK, GM_GROUPS, GM_GC)
    s = jnp.einsum('gpq,bnqgc->bnpgc', w_s, v) + b_s.T[:, :, None]
    return gu * s.reshape(b, n, GM_WIDTH)

def ec_moe(h, w_router, w_e1, w_e3, w_e2):
    b, n, d = h.shape
    cap = EC_FACTOR * n // N_EXPERTS
    aff = jax.nn.softmax((h @ w_router).astype(jnp.float32), axis=-1)
    gate, idx = lax.top_k(jnp.swapaxes(aff, 1, 2), cap)
    xg = jax.vmap(lambda hb, ib: hb[ib])(h, idx)
    a = jnp.einsum('becd,edf->becf', xg, w_e1)
    g3 = jnp.einsum('becd,edf->becf', xg, w_e3)
    y = jnp.einsum('becf,efd->becd', jax.nn.silu(a) * g3, w_e2) * gate[..., None].astype(h.dtype)
    return jax.vmap(lambda yb, ib: jnp.zeros((n, d), yb.dtype).at[ib.reshape(-1)].add(yb.reshape(-1, d)))(y, idx)

def trunk_layer(x, mod, p, ang, ctx):
    b, n, _ = x.shape
    sh1, sc1, gate1, sh2, sc2, gate2 = jnp.split(mod, 6, axis=-1)
    h = rms(x, p['g_attn']) * (1 + sc1) + sh1
    cuts = list(np.cumsum(IN_SPLITS)[:-1])
    q_a, kv_c, k_r, gu, gv, ga, gb = jnp.split(h @ p['w_in'], cuts, axis=-1)
    q = (rms(q_a, p['g_qa']) @ p['w_qb']).reshape(b, n, N_HEADS, D_NOPE + D_ROPE)
    q_nope, q_rope = q[..., :D_NOPE], q[..., D_NOPE:]
    ckv = rms(kv_c, p['g_kv'])
    if ang is not None:
        q_rope = apply_rope2d(q_rope, ang[:, None])
        k_r = apply_rope2d(k_r, ang)
    k_all, kr_all = ckv, k_r
    if ctx is not None:
        k_all = jnp.concatenate([ckv, ctx[0]], axis=1)
        kr_all = jnp.concatenate([k_r, ctx[1]], axis=1)
    k_nope = jnp.einsum('bkr,rhd->bkhd', k_all, p['w_uk'])
    v = jnp.einsum('bkr,rhd->bkhd', k_all, p['w_uv'])
    o_a = attend(q_nope, q_rope, k_nope, kr_all, v) @ p['w_o_mla']
    o_b = spatial_gating(jax.nn.gelu(gu), jax.nn.gelu(gv), p['g_sgu'], p['w_s'], p['b_s']) @ p['w_o_gm']
    merged = jax.nn.sigmoid(ga) * o_a + jax.nn.sigmoid(gb) * o_b
    x = x + gate1 * (merged @ p['w_out'])
    h2 = rms(x, p['g_ffn']) * (1 + sc2) + sh2
    x = x + gate2 * ec_moe(h2, p['w_router'], p['w_e1'], p['w_e3'], p['w_e2'])
    return x, ckv, k_r

def setup_inputs(seed: int = 0) -> dict:
    key = jax.random.key(seed)
    ks = jax.random.split(key, 32)
    f = jnp.float32
    nrm = lambda k, shape, s: jax.random.normal(k, shape, f) * s
    L, D, H = DEPTH, D_MODEL, N_HEADS
    return {
        'x_prompt': nrm(ks[0], (BATCH, SEQ, D), 1.0),
        'x_sample': nrm(ks[1], (DEC_BATCH, DEC_SEQ, D), 1.0),
        'c': nrm(ks[2], (DEC_BATCH, D), 1.0),
        'cache_ckv': nrm(ks[3], (DEC_BATCH, L, PAST_LEN, KV_LORA), 1.0),
        'cache_krope': nrm(ks[4], (DEC_BATCH, L, PAST_LEN, D_ROPE), 1.0),
        'c_ctx': nrm(ks[5], (D,), 1.0),
        'g_attn': 1.0 + nrm(ks[6], (L, D), 0.02),
        'g_ffn': 1.0 + nrm(ks[7], (L, D), 0.02),
        'w_ada': nrm(ks[8], (L, D, 6 * D), 0.5 * D ** -0.5),
        'b_ada': nrm(ks[9], (L, 6 * D), 0.02),
        'w_in': nrm(ks[10], (L, D, IN_WIDTH), D ** -0.5),
        'g_qa': 1.0 + nrm(ks[11], (L, Q_LORA), 0.02),
        'w_qb': nrm(ks[12], (L, Q_LORA, H * (D_NOPE + D_ROPE)), Q_LORA ** -0.5),
        'g_kv': 1.0 + nrm(ks[13], (L, KV_LORA), 0.02),
        'w_uk': nrm(ks[14], (L, KV_LORA, H, D_NOPE), KV_LORA ** -0.5),
        'w_uv': nrm(ks[15], (L, KV_LORA, H, D_V), KV_LORA ** -0.5),
        'w_o_mla': nrm(ks[16], (L, H * D_V, D), (H * D_V) ** -0.5),
        'g_sgu': 1.0 + nrm(ks[17], (L, GM_WIDTH), 0.02),
        'w_s': nrm(ks[18], (L, GM_GROUPS, CHUNK, CHUNK), CHUNK ** -0.5),
        'b_s': 1.0 + nrm(ks[19], (L, GM_GROUPS, CHUNK), 0.02),
        'w_o_gm': nrm(ks[20], (L, GM_WIDTH, D), GM_WIDTH ** -0.5),
        'w_out': nrm(ks[21], (L, D, D), D ** -0.5),
        'w_router': nrm(ks[22], (L, D, N_EXPERTS), D ** -0.5),
        'w_e1': nrm(ks[23], (L, N_EXPERTS, D, D_FF_EXPERT), D ** -0.5),
        'w_e3': nrm(ks[24], (L, N_EXPERTS, D, D_FF_EXPERT), D ** -0.5),
        'w_e2': nrm(ks[25], (L, N_EXPERTS, D_FF_EXPERT, D), D_FF_EXPERT ** -0.5),
        'g_final': 1.0 + nrm(ks[26], (D,), 0.02),
    }

def reference(x_prompt, x_sample, c, cache_ckv, cache_krope, c_ctx,
              g_attn, g_ffn, w_ada, b_ada, w_in, g_qa, w_qb, g_kv, w_uk, w_uv, w_o_mla,
              g_sgu, w_s, b_s, w_o_gm, w_out, w_router, w_e1, w_e3, w_e2, g_final):
    ang = rope_angles(x_sample.shape[1])
    xc, xl = x_prompt, x_sample
    ckv_list, kr_list = [], []
    for l in range(DEPTH):
        p = dict(g_attn=g_attn[l], g_ffn=g_ffn[l], w_in=w_in[l], g_qa=g_qa[l], w_qb=w_qb[l],
                 g_kv=g_kv[l], w_uk=w_uk[l], w_uv=w_uv[l], w_o_mla=w_o_mla[l], g_sgu=g_sgu[l],
                 w_s=w_s[l], b_s=b_s[l], w_o_gm=w_o_gm[l], w_out=w_out[l], w_router=w_router[l],
                 w_e1=w_e1[l], w_e3=w_e3[l], w_e2=w_e2[l])
        mod_ctx = jax.nn.silu(c_ctx) @ w_ada[l] + b_ada[l]
        mod_lat = (jax.nn.silu(c) @ w_ada[l] + b_ada[l])[:, None, :]
        xc, ckv_c, kr_c = trunk_layer(xc, mod_ctx, p, None, None)
        ckv_list.append(ckv_c)
        kr_list.append(kr_c)
        xl, _, _ = trunk_layer(xl, mod_lat, p, ang, (cache_ckv[:, l], cache_krope[:, l]))
    y_prompt = rms(xc, g_final)
    y_sample = rms(xl, g_final)
    new_ckv = jnp.stack(ckv_list, axis=1)
    new_krope = jnp.stack(kr_list, axis=1)
    return (y_prompt, y_sample, new_ckv, new_krope)


_drawn_inputs = setup_inputs


def setup_inputs(seed=0):
    import zlib

    import numpy as np

    out = dict(_drawn_inputs(seed))
    spreads = {}
    factors = {'cache_ckv': 8.0,
     'cache_krope': 8.0,
     'g_attn': 2.893,
     'g_ffn': 8.0,
     'g_qa': 8.0,
     'w_qb': 2.703,
     'g_kv': 2.708,
     'w_uk': 3.105,
     'g_sgu': 8.0,
     'b_s': 8.0,
     'g_final': 2.896}
    for name, (base, spread) in spreads.items():
        noise = np.random.default_rng([zlib.crc32(name.encode()), seed]).standard_normal(out[name].shape)
        drawn = base * np.exp(spread * noise) if base else spread * noise
        out[name] = __import__('jax').numpy.asarray(drawn.astype(out[name].dtype))
    for name, factor in factors.items():
        out[name] = (out[name] * factor).astype(out[name].dtype)
    return out
```

```python
from contextlib import ExitStack

import numpy as np

import concourse.bass as bass
from concourse import mybir

ALU = mybir.AluOpType
ACT = mybir.ActivationFunctionType
AX = mybir.AxisListType
F32 = mybir.dt.float32
F32R = mybir.dt.float32r
U32 = mybir.dt.uint32

P = 128
D = 2048
KT = D // P
N_CTX, N_LAT = 128, 512
N_TOK = N_CTX + N_LAT
TT = N_TOK // P
N_PAST = 256
Q_LORA, KV_LORA, D_ROPE = 512, 256, 64
HEADS, D_NOPE, D_V = 16, 128, 128
D_Q = D_NOPE + D_ROPE
ROPE_FREQS = D_ROPE // 4
IN_WIDTH = Q_LORA + KV_LORA + D_ROPE + 4 * D
KVR = KV_LORA + D_ROPE
GROUPS, GC = 8, D // 8
EXPERTS, D_FF = 16, D // 2
CAP_LAT, CAP_CTX = 2 * N_LAT // EXPERTS, 2 * N_CTX // EXPERTS
SLOTS = CAP_LAT + CAP_CTX
NC = 512
KG = 4
PIECE = KG * NC
EPS = 1e-6
KEYT = (N_TOK + N_PAST) // P
N_KEY = KEYT * P
LAT_KEYS = N_KEY - N_CTX
SM_SCALE = float(D_NOPE + D_ROPE) ** -0.5
SBUF_FROM, SBUF_TO = 16512, 229344


class Names:
    pass


class Stream:

    def __init__(self, sem, name, n_stage, n_w):
        self.landed = [sem(f"{name}_landed{s}") for s in range(n_stage)]
        self.hi, self.split, self.used = sem(f"{name}_hi"), sem(f"{name}_split"), sem(f"{name}_used")
        self.n_stage, self.n_w = n_stage, n_w


class Map:

    def __init__(self, nc, at):
        self.nc, self.at = nc, at

    def new(self, name, shape, dtype):
        size = 4 * int(np.prod(shape[1:]))
        t = self.nc.alloc_sbuf_tensor_at(name, list(shape), dtype, offset=self.at)
        self.at += (size + 31) // 32 * 32
        assert self.at <= SBUF_TO, (name, self.at)
        return t


def phase_semaphores(ctx, nc):
    made = []

    def release():
        nc.clear_and_free_semaphores(made)
        nc.all_engine_barrier()
    ctx.callback(release)

    def sem(name):
        made.append(nc.alloc_semaphore(name))
        return made[-1]
    return sem


def load_piece(sp, st, n, slot, dst, src):
    sp.wait_ge(st.split, n + 1)
    sp.dma_start(dst, src).then_inc(st.landed[slot], 16)


def piece_hi(act, st, n, slot, uses, dst, src):
    act.wait_ge(st.landed[slot], 16 * uses)
    act.wait_ge(st.used, n + 1)
    act.activation(dst, src, ACT.Copy).then_inc(st.hi, 1)


def piece_lo(dve, st, n, dst, src, hi):
    dve.wait_ge(st.hi, n + 1)
    dve.tensor_tensor(dst, src, hi.bitcast(F32), ALU.subtract).then_inc(st.split, 1)


def product(pe, out, x_hi, x_lo, w_hi, w_lo, first, last):
    pe.matmul(out, x_hi, w_hi, start=first, stop=False)
    pe.matmul(out, x_hi, w_lo, start=False, stop=False)
    return pe.matmul(out, x_lo, w_hi, start=False, stop=last)


def phase_modulate(nc, M, I, W):
    m = Map(nc, M.phase_at)
    hT_at = m.at
    M.hT_hi = m.new("hT_hi", [P, KT, N_TOK], F32R)
    M.hT_lo = m.new("hT_lo", [P, KT, N_TOK], F32R)
    M.hT_end = m.at
    raw = Map(nc, hT_at)
    x_row = [raw.new(f"x_row{b}", [P, D], F32) for b in range(2)]
    square = raw.new("x_square", [P, D], F32)
    xT = m.new("xT", [P, KT, N_TOK], F32)
    cvec = m.new("cvec", [P, 2, KT], F32)
    csil = m.new("csil", [P, 2, KT], F32)
    c_st = M.c_st
    spare = Map(nc, W.spare_at)
    low_rows = spare.new("low_rows", [2, NC], F32)
    mod_row = spare.new("mod_row", [2, NC], F32)
    b_row = spare.new("b_row", [2, 1, NC], F32)
    vec_rows = m.new("vec_rows", [80, P], F32)
    cols = m.new("mod_cols", [P, 80], F32)
    gain = m.new("mod_gain", [P, 32], F32)
    st = m.new("x_stats", [P, 4, TT], F32)
    xm = m.new("x_mod", [P, N_TOK], F32)

    with ExitStack() as ctx:
        sem = phase_semaphores(ctx, nc)
        ps = [ctx.enter_context(nc.psum_tensor(f"m_ps{b}", [P, NC], F32)) for b in range(8)]
        s = Stream(sem, "ada", 4, 2)
        passed = sem("pool_passed")
        ident0, ident_ok, small_in, small_cols = sem("ident0"), sem("ident_ok"), sem("small_in"), sem("small_cols")
        x_in = [sem("x_in0"), sem("x_in1")]
        x_sq, x_var, x_std, x_inv, x_hat, x_tr, x_ev = (sem(n) for n in ("x_sq", "x_var", "x_std", "x_inv", "x_hat", "x_tr", "x_ev"))
        c_sil, c_zero, c_hi, c_lo = sem("c_sil"), sem("c_zero"), sem("c_hi"), sem("c_lo")
        ada_low, ada_sum, ada_row, row_free = (sem(n) for n in ("ada_low", "ada_sum", "ada_row", "row_free"))
        b_in, mod_out, vec_in = (M.pool_sem(n) for n in ("b_in", "mod_out", "vec_in"))
        vec_tr, vec_cols, gain_ok, mod_hi, mod_val, mod_done = (sem(n) for n in ("vec_tr", "vec_cols", "gain_ok", "mod_hi", "mod_val", "mod_done"))
        block = ctx.enter_context(nc.Block())
        ADA = I["w_ada"].rearrange("l (p g j) n -> (l g) p j n", g=KG, j=KG)

        @block.sync
        def _(sp):
            sp.dma_start(cvec[:, 0, :], I["c_ctx"].rearrange("(p t) -> p t", p=P)).then_inc(small_in, 16)
            sp.dma_start(cvec[:, 1, :], I["c"].rearrange("b (p t) -> p (b t)", p=P)).then_inc(small_in, 16)
            for t in range(TT):
                if t >= 2:
                    sp.wait_ge(x_tr, 4 * (t - 1))
                sp.dma_start(x_row[t % 2][:], x_tile(I, t)).then_inc(x_in[t % 2], 16)
            with sp.Fori(0, 2 * D // NC) as i:
                for g in range(KG):
                    load_piece(sp, s, 4 * i + g, g, W.stage[:, g, :].rearrange("p (j n) -> p j n", j=KG),
                               ADA[g][:, :, bass.ds(i * NC, NC)])

        @block.gpsimd
        def _(pool):
            pool.memset(M.ident[:], 0.0).then_inc(ident0, 1)
            pool.wait_ge(ident0, 1)
            pool.affine_select(out=M.ident[:], in_=M.ident[:], compare_op=ALU.not_equal, fill=1.0, base=0,
                               pattern=[[-1, P]], channel_multiplier=1).then_inc(ident_ok, 1)
            ada_chunks(pool, I, M, b_row, mod_row, ada_row, ada_sum, b_in, mod_out, row_free, passed, 0, 2 * D // NC)
            pool.wait_ge(mod_out, 16 * (2 * D // NC))
            for r in range(2):
                pool.dma_start(vec_rows[32 * r:32 * r + 32, :],
                               M.mod[r, 0:2 * D].rearrange("(k p) -> k p", p=P)).then_inc(vec_in, 16)
            pool.dma_start(vec_rows[64:80, :], I["g_attn"].rearrange("l (k p) -> (l k) p", p=P)).then_inc(vec_in, 16)
            pool.wait_ge(vec_in, 48)

        @block.scalar
        def _(act):
            act.wait_ge(small_in, 32)
            act.activation(csil[:], cvec[:], ACT.Silu).then_inc(c_sil, 1)
            act.wait_ge(c_sil, 1)
            act.wait_ge(c_zero, 1)
            act.activation(c_st[:, :, 0:2], csil[:].rearrange("p s t -> p t s"), ACT.Copy).then_inc(c_hi, 1)
            for t in range(TT):
                act.wait_ge(x_in[t % 2], 16 * (t // 2 + 1))
                if t:
                    act.wait_ge(x_sq, t)
                act.activation(square[:], x_row[t % 2][:], ACT.Square, accum_out=st[:, 0, t:t + 1]).then_inc(x_sq, 1)
                act.wait_ge(x_var, t + 1)
                act.activation(st[:, 2, t:t + 1], st[:, 1, t:t + 1], ACT.Sqrt).then_inc(x_std, 1)
                for q in range(4):
                    act.wait_ge(x_tr, 4 * t + q + 1)
                    act.activation(xT[:, 4 * q:4 * q + 4, bass.ts(t, P)], ps[1 + q][:].rearrange("p (j n) -> p j n", j=4),
                                   ACT.Copy).then_inc(x_ev, 1)
            with act.Fori(0, 2 * D // NC) as i:
                for g in range(KG):
                    piece_hi(act, s, 4 * i + g, g, i + 1, W.hi[:, g % 2, :], W.stage[:, g, :])
                act.wait_ge(s.used, s.n_w + 4 * i + 4)
                act.wait_ge(ada_sum, i + 1)
                act.activation(low_rows[:], ps[0][32:34, :], ACT.Copy).then_inc(ada_low, 1)
            act.wait_ge(gain_ok, 1)
            for k in range(KT):
                for r, (a, b) in enumerate(((0, N_CTX), (N_CTX, N_TOK))):
                    act.activation(M.hT_hi[:, k, a:b], xT[:, k, a:b], ACT.Identity, scale=gain[:, 16 * r + k:16 * r + k + 1],
                                   bias=cols[:, 32 * r + k:32 * r + k + 1]).then_inc(mod_hi, 1)

        @block.vector
        def _(dve):
            dve.sem_inc(s.split, s.n_stage)
            dve.sem_inc(ada_sum, 1)
            dve.memset(c_st[:].bitcast(F32), 0.0).then_inc(c_zero, 1)
            dve.wait_ge(c_sil, 1)
            dve.wait_ge(c_hi, 1)
            dve.tensor_tensor(c_st[:, :, 32:34], csil[:].rearrange("p s t -> p t s"), c_st[:, :, 0:2].bitcast(F32),
                              ALU.subtract).then_inc(c_lo, 1)
            for t in range(TT):
                dve.wait_ge(x_sq, t + 1)
                dve.tensor_scalar(st[:, 1, t:t + 1], st[:, 0, t:t + 1], 1.0 / D, EPS, ALU.mult, ALU.add).then_inc(x_var, 1)
                dve.wait_ge(x_std, t + 1)
                dve.reciprocal(st[:, 3, t:t + 1], st[:, 2, t:t + 1]).then_inc(x_inv, 1)
                dve.wait_ge(x_inv, t + 1)
                dve.tensor_scalar(x_row[t % 2][:], x_row[t % 2][:], st[:, 3, t:t + 1], None, ALU.mult).then_inc(x_hat, 1)
            with dve.Fori(0, 2 * D // NC) as i:
                for g in range(KG):
                    piece_lo(dve, s, 4 * i + g, W.lo[:, g % 2, :], W.stage[:, g, :], W.hi[:, g % 2, :])
                ada_sum_rows(dve, i, low_rows, mod_row, b_row, ps[0], ada_low, ada_sum, ada_row, b_in, row_free)
            dve.wait_ge(vec_tr, 1)
            dve.tensor_copy(cols[:], ps[1][:, 0:80]).then_inc(vec_cols, 1)
            dve.wait_ge(vec_cols, 1)
            for r in range(2):
                ins = dve.scalar_tensor_tensor(gain[:, 16 * r:16 * r + 16], cols[:, 32 * r + 16:32 * r + 32], 1.0,
                                               cols[:, 64:80], ALU.add, ALU.mult)
            ins.then_inc(gain_ok, 1)
            dve.wait_ge(gain_ok, 1)
            for k in range(KT):
                if k:
                    dve.wait_ge(mod_done, k)
                for r, (a, b) in enumerate(((0, N_CTX), (N_CTX, N_TOK))):
                    dve.tensor_scalar(xm[:, a:b], xT[:, k, a:b], gain[:, 16 * r + k:16 * r + k + 1],
                                      cols[:, 32 * r + k:32 * r + k + 1], ALU.mult, ALU.add).then_inc(mod_val, 1)
                dve.wait_ge(mod_val, 2 * k + 2)
                dve.wait_ge(mod_hi, 2 * k + 2)
                dve.tensor_tensor(M.hT_lo[:, k, :], xm[:], M.hT_hi[:, k, :].bitcast(F32), ALU.subtract).then_inc(mod_done, 1)

        @block.tensor
        def _(pe):
            pe.sem_inc(s.used, s.n_w)
            pe.wait_ge(ident_ok, 1)
            for t in range(TT):
                pe.wait_ge(x_hat, t + 1)
                for q in range(4):
                    if t:
                        pe.wait_ge(x_ev, 4 * (t - 1) + q + 1)
                    for j in range(4):
                        ins = pe.transpose(ps[1 + q][:, bass.ts(j, P)], x_row[t % 2][:, bass.ts(4 * q + j, P)], M.ident[:])
                    ins.then_inc(x_tr, 1)
            pe.wait_ge(c_lo, 1)
            with pe.Fori(0, 2 * D // NC) as i:
                ada_products(pe, s, i, W, c_st, ps[0], ada_row, lambda g: g % 2)
            pe.wait_ge(vec_in, 48)
            pe.wait_ge(x_ev, 4 * TT)
            pe.transpose(ps[1][:, 0:80], vec_rows[:], M.ident[0:80, 0:80]).then_inc(vec_tr, 1)


def pool_wait(pool, sem, value, passed):
    pool.wait_ge(sem, value)
    pool.sem_inc(passed, 1)


def x_tile(I, t):
    return I["x_prompt"][0] if t == 0 else I["x_sample"][0, bass.ts(t - 1, P), :]


def ada_piece(pe, s, n, g, W, wslot, c_st, out):
    pe.wait_ge(s.split, n + 1 + s.n_stage)
    for j in range(KG):
        k = KG * g + j
        with_hi = lambda: pe.matmul(out[0:34, :], c_st[:, k, 0:34], W.hi[:, wslot, bass.ts(j, NC)], start=(k == 0),
                                    stop=(k == KT - 1), skip_group_check=True)
        if k < KT - 1:
            with_hi()
        ins = pe.matmul(out[0:2, :], c_st[:, k, 0:2], W.lo[:, wslot, bass.ts(j, NC)], start=False, stop=False,
                        skip_group_check=True)
        if k == KT - 1:
            ins = with_hi()
    ins.then_inc(s.used, 1)


def ada_products(pe, s, i, W, c_st, out, ada_row, wslot):
    pe.wait_ge(ada_row, i + 1)
    for g in range(KG):
        ada_piece(pe, s, 4 * i + g, g, W, wslot(g), c_st, out)


def ada_chunks(pool, I, M, b_row, mod_row, ada_row, ada_sum, b_in, mod_out, row_free, passed, c0, n):
    pool.sem_inc(ada_row, 1)
    pool.sem_inc(row_free, 1)
    B = I["b_ada"]
    with pool.Fori(0, n) as i:
        pool_wait(pool, ada_row, i + 1, passed)
        pool.dma_start(b_row[:, 0, :], B[:, bass.ds((i + c0) * NC, NC)].to_broadcast((2, NC))).then_inc(b_in, 16)
        pool_wait(pool, ada_row, i + 2, passed)
        pool.dma_start(M.mod[:, bass.ds((i + c0) * NC, NC)], mod_row[:]).then_inc(mod_out, 16)
        pool_wait(pool, mod_out, 16 * i + 16, row_free)


def ada_sum_rows(dve, i, low_rows, mod_row, b_row, out, ada_low, ada_sum, ada_row, b_in, row_free):
    dve.wait_ge(ada_low, i + 1)
    dve.wait_ge(row_free, i + 1)
    dve.tensor_tensor(mod_row[:], out[0:2, :], low_rows[:], ALU.add).then_inc(ada_sum, 1)
    dve.wait_ge(ada_sum, i + 2)
    dve.wait_ge(b_in, 16 * i + 16)
    dve.tensor_tensor(mod_row[:], mod_row[:], b_row[:, 0, :], ALU.add).then_inc(ada_row, 1)


def dense_piece(pe, st, n, g, wslot, W, x_hi, x_lo, acc, acc_ready, acc_free, evacuated, width=NC):
    pe.wait_ge(st.split, n + 1 + st.n_stage)
    for t in range(TT):
        if g == 0 and evacuated is not None:
            pe.wait_ge(acc_free, evacuated + t + 1)
        for j in range(KG):
            k = KG * g + j
            ins = product(pe, acc[t][:, 0:width], x_hi[:, k, bass.ts(t, P)], x_lo[:, k, bass.ts(t, P)],
                          W.hi[:, wslot, bass.ts(j, width)], W.lo[:, wslot, bass.ts(j, width)], k == 0, k == KT - 1)
        if g == KG - 1 and t < TT - 1:
            ins.then_inc(acc_ready, 1)
    ins.then_inc(st.used, 1)


def wait_acc(engine, st, acc_ready, c, t):
    if t < TT - 1:
        engine.wait_ge(acc_ready, (TT - 1) * c + t + 1)
    else:
        engine.wait_ge(st.used, st.n_w + KG * c + KG)


def phase_in_proj(nc, M, I, W):
    m = Map(nc, M.hT_end)
    M.qa = m.new("q_a", [P, TT, Q_LORA], F32)
    M.kvr = m.new("kv_and_rope", [P, TT, KVR], F32)
    ev = m.new("evacuated", [P, TT, NC], F32)
    low_rows = m.new("low_rows2", [2, NC], F32)
    mod_row = m.new("mod_row2", [2, NC], F32)
    b_row = m.new("b_row2", [2, 1, NC], F32)
    N_CH = 4 * D // NC
    ADA0 = 2 * D // NC
    W_IN = I["w_in"].rearrange("l (g j p) n -> (l g) p j n", g=KG, j=KG)
    ADA = I["w_ada"].rearrange("l (p g j) n -> (l g) p j n", g=KG, j=KG)
    W0 = Q_LORA + KVR

    with ExitStack() as ctx:
        sem = phase_semaphores(ctx, nc)
        ps = [ctx.enter_context(nc.psum_tensor(f"i_ps{b}", [P, NC], F32)) for b in range(6)]
        d, a = Stream(sem, "in", 2, 2), Stream(sem, "ada2", 2, 1)
        acc_ready, acc_free, stored = sem("in_acc_ready"), sem("in_acc_free"), sem("in_stored")
        st_sem = [M.pool_sem(f"in_store{t}") for t in range(TT)]
        b_in, mod_out = M.pool_sem("i_b_in"), M.pool_sem("i_mod_out")
        passed, ada_low, ada_sum, ada_row, row_free = (
            sem(n) for n in ("i_passed", "i_ada_low", "i_ada_sum", "i_ada_row", "i_row_free"))
        block = ctx.enter_context(nc.Block())

        def stage(slot, width=NC):
            return W.stage[:, slot, 0:KG * width]

        @block.sync
        def _(sp):
            for c, (c0, width) in enumerate(((0, Q_LORA), (Q_LORA, KVR))):
                for g in range(KG):
                    load_piece(sp, d, KG * c + g, g % 2, stage(g % 2, width).rearrange("p (j n) -> p j n", j=KG),
                               W_IN[g][:, :, c0:c0 + width])
            with sp.Fori(0, N_CH) as i:
                for g in range(KG):
                    load_piece(sp, d, 2 * KG + KG * i + g, g % 2, stage(g % 2).rearrange("p (j n) -> p j n", j=KG),
                               W_IN[g][:, :, bass.ds(i * NC + W0, NC)])
                    load_piece(sp, a, KG * i + g, g % 2, stage(2 + g % 2).rearrange("p (j n) -> p j n", j=KG),
                               ADA[g][:, :, bass.ds((i + ADA0) * NC, NC)])

        @block.gpsimd
        def _(pool):
            pool.sem_inc(ada_row, 1)
            pool.sem_inc(row_free, 1)
            pool.sem_inc(stored, TT)
            B = I["b_ada"]
            with pool.Fori(0, N_CH) as i:
                pool_wait(pool, ada_row, i + 1, passed)
                pool.dma_start(b_row[:, 0, :], B[:, bass.ds((i + ADA0) * NC, NC)].to_broadcast((2, NC))).then_inc(b_in, 16)
                for t in range(TT):
                    pool_wait(pool, acc_free, TT * (i + 2) + t + 1, passed)
                    pool.dma_start(M.acts[bass.ts(t, P), bass.ds(i * NC, NC)], ev[:, t, :]).then_inc(st_sem[t], 16)
                for t in range(TT):
                    pool_wait(pool, st_sem[t], 16 * i + 16, stored)
                pool_wait(pool, ada_row, i + 2, passed)
                pool.dma_start(M.mod[:, bass.ds((i + ADA0) * NC, NC)], mod_row[:]).then_inc(mod_out, 16)
                pool_wait(pool, mod_out, 16 * i + 16, row_free)

        @block.scalar
        def _(act):
            def weights(i):
                for g in range(KG):
                    piece_hi(act, a, KG * i + g, g % 2, 2 * i + g // 2 + 1, W.hi[:, 2, :], stage(2 + g % 2))
                    if g < KG - 1:
                        dense_hi(i, g + 1)

            def dense_hi(i, g):
                piece_hi(act, d, 2 * KG + KG * i + g, g % 2, KG + 2 * i + g // 2 + 1, W.hi[:, g % 2, :], stage(g % 2))

            def evacuate(i, func):
                for t in range(TT):
                    wait_acc(act, d, acc_ready, i + 2, t)
                    act.wait_ge(stored, TT * i + t + 1)
                    act.activation(ev[:, t, :], ps[t][:], func).then_inc(acc_free, 1)
                act.wait_ge(a.used, a.n_w + KG * i + KG)
                act.wait_ge(ada_sum, i + 1)
                act.activation(low_rows[:], ps[5][32:34, :], ACT.Copy).then_inc(ada_low, 1)

            for c, width in enumerate((Q_LORA, KVR)):
                for g in range(KG):
                    piece_hi(act, d, KG * c + g, g % 2, 2 * c + g // 2 + 1, W.hi[:, g % 2, 0:KG * width], stage(g % 2, width))
                if c:
                    dense_hi(0, 0)
                for t in range(TT):
                    wait_acc(act, d, acc_ready, c, t)
                    act.activation((M.kvr if c else M.qa)[:, t, :], ps[t][:, 0:width], ACT.Copy).then_inc(acc_free, 1)
            weights(0)
            with act.Fori(1, N_CH // 2) as i:
                dense_hi(i, 0)
                evacuate(i - 1, ACT.Gelu_apprx_tanh)
                weights(i)
            dense_hi(N_CH // 2, 0)
            evacuate(N_CH // 2 - 1, ACT.Gelu_apprx_tanh)
            weights(N_CH // 2)
            with act.Fori(N_CH // 2 + 1, N_CH) as i:
                dense_hi(i, 0)
                evacuate(i - 1, ACT.Sigmoid)
                weights(i)
            evacuate(N_CH - 1, ACT.Sigmoid)

        @block.vector
        def _(dve):
            dve.sem_inc(d.split, d.n_stage)
            dve.sem_inc(a.split, a.n_stage)
            dve.sem_inc(ada_sum, 1)

            def dense_lo(n, g, width=NC):
                piece_lo(dve, d, n, W.lo[:, g % 2, 0:KG * width], stage(g % 2, width), W.hi[:, g % 2, 0:KG * width])

            def weights(i):
                for g in range(KG):
                    piece_lo(dve, a, KG * i + g, W.lo[:, 2, :], stage(2 + g % 2), W.hi[:, 2, :])
                    if g < KG - 1:
                        dense_lo(2 * KG + KG * i + g + 1, g + 1)

            for c, width in enumerate((Q_LORA, KVR)):
                for g in range(KG):
                    dense_lo(KG * c + g, g, width)
            dense_lo(2 * KG, 0)
            weights(0)
            with dve.Fori(1, N_CH) as i:
                dense_lo(2 * KG + KG * i, 0)
                ada_sum_rows(dve, i - 1, low_rows, mod_row, b_row, ps[5], ada_low, ada_sum, ada_row, b_in, row_free)
                weights(i)
            ada_sum_rows(dve, N_CH - 1, low_rows, mod_row, b_row, ps[5], ada_low, ada_sum, ada_row, b_in, row_free)

        @block.tensor
        def _(pe):
            pe.sem_inc(d.used, d.n_w)
            pe.sem_inc(a.used, a.n_w)
            x = (M.hT_hi, M.hT_lo, ps, acc_ready, acc_free)
            for c, width in enumerate((Q_LORA, KVR)):
                for g in range(KG):
                    dense_piece(pe, d, KG * c + g, g, g % 2, W, *x, 0 if c else None, width)
            with pe.Fori(0, N_CH) as i:
                for g in range(KG):
                    dense_piece(pe, d, 2 * KG + KG * i + g, g, g % 2, W, *x, TT * (i + 1))
                    if g == 0:
                        pe.wait_ge(ada_row, i + 1)
                    ada_piece(pe, a, KG * i + g, g, W, 2, M.c_st, ps[5])


def phase_mix(nc, M, I, W, O):
    m = Map(nc, M.phase_at)
    M.qaT_hi, M.qaT_lo = (m.new(f"qaT_{h}", [P, KG, N_TOK], F32R) for h in ("hi", "lo"))
    M.ckvT = m.new("ckvT", [P, 2, N_KEY], F32)
    M.ckvT_hi, M.ckvT_lo = (m.new(f"ckvT_{h}", [P, 2, N_KEY], F32R) for h in ("hi", "lo"))
    M.krT_hi, M.krT_lo = (m.new(f"krT_{h}", [D_ROPE, N_KEY], F32R) for h in ("hi", "lo"))
    M.heads_at = m.at
    ckv = m.new("ckv", [P, KEYT, KV_LORA], F32)
    kr = m.new("kr", [P, KEYT, D_ROPE], F32)
    kr_cos = m.new("kr_cos", [P, TT, D_ROPE], F32)
    kr_sin = m.new("kr_sin", [P, TT, D_ROPE], F32)
    table = m.new("rope_rows_sb", [P, TT, 2 * D_ROPE], F32)
    st = m.new("qk_stats", [P, 4, 2 * TT], F32)
    gst = m.new("gm_stats", [P, 4, TT], F32)
    assert m.at <= M.hT_end
    m = Map(nc, M.hT_end + 4 * TT * (Q_LORA + KVR))
    g_q = m.new("g_q", [P, Q_LORA], F32)
    g_kv = m.new("g_kv_rows", [P, KV_LORA], F32)
    g_gm = m.new("g_gm", [P, D], F32)
    ws = m.new("ws", [P, GROUPS, P], F32)
    wsT = m.new("wsT", [P, GROUPS, P], F32)
    b_rows = m.new("b_rows", [GROUPS, P], F32)
    b_col = m.new("b_col", [P, GROUPS], F32)
    square = m.new("gm_square", [P, D], F32)
    m = Map(nc, W.at)
    gv = [m.new(f"gv{b}", [P, D], F32) for b in range(2)]
    gu = [m.new(f"gu{b}", [P, D], F32) for b in range(2)]
    mixed = m.new("gm_mixed", [P, D], F32)
    turned = [m.new(f"gm_turned{b}", [P, KT, P], F32) for b in range(2)]
    assert m.at <= M.phase_at

    with ExitStack() as ctx:
        sem = phase_semaphores(ctx, nc)
        ps = [ctx.enter_context(nc.psum_tensor(f"x_ps{b}", [P, NC], F32)) for b in range(8)]
        consts, ctx_out = M.pool_sem("c3_consts"), M.pool_sem("ctx_out")
        sq, var, std, inv, q_hat, kv_hat, rot_part, rot = (sem(f"c3_{n}") for n in ("sq", "var", "std", "inv", "q_hat", "kv_hat", "rot_part", "rot"))
        q_tr, q_hi, q_lo, kv_tr, kv_f, kv_hi, kv_lo, kr_tr, kr_hi, kr_lo = (
            sem(f"c3_{n}") for n in ("q_tr", "q_hi", "q_lo", "kv_tr", "kv_f", "kv_hi", "kv_lo", "kr_tr", "kr_hi", "kr_lo"))
        ws_tr, ws_ev, acts_in = sem("ws_tr"), sem("ws_ev"), [sem("acts_in0"), sem("acts_in1")]
        g_sq, g_var, g_std, g_inv, g_hat, g_mm, g_mix, g_tr, g_ev = (
            sem(f"gm_{n}") for n in ("sq", "var", "std", "inv", "hat", "mm", "mix", "tr", "ev"))
        g_out = [sem("gm_out0"), sem("gm_out1")]
        block = ctx.enter_context(nc.Block())
        OBT = M.obT.rearrange("(k p) n -> p k n", p=P)
        quad = lambda ap: ap.rearrange("p t (a h f) -> p t a h f", a=2, h=2)
        N_CONST = 8

        @block.sync
        def _(sp):
            for t in range(TT):
                if t >= 2:
                    sp.wait_ge(g_mm, t - 1)
                    sp.wait_ge(g_mix, t - 1)
                sp.dma_start(gu[t % 2][:], M.acts[bass.ts(t, P), 0:D]).then_inc(acts_in[t % 2], 16)
                sp.dma_start(gv[t % 2][:], M.acts[bass.ts(t, P), D:2 * D]).then_inc(acts_in[t % 2], 16)
            for t in range(TT):
                sp.wait_ge(g_ev, 4 * t + 4)
                sp.dma_start(OBT[:, :, bass.ts(t, P)], turned[t % 2][:]).then_inc(g_out[t % 2], 16)
            sp.wait_ge(g_out[0], 16 * ((TT + 1) // 2))
            sp.wait_ge(g_out[1], 16 * (TT // 2))

        @block.gpsimd
        def _(pool):
            past = lambda x: x[0, 0].rearrange("(t p) n -> p t n", p=P)
            for dst, src in ((g_q[:], I["g_qa"].to_broadcast((P, Q_LORA))), (g_kv[:], I["g_kv"].to_broadcast((P, KV_LORA))),
                             (ckv[:, TT:KEYT, :], past(I["cache_ckv"])), (kr[:, TT:KEYT, :], past(I["cache_krope"])),
                             (table[:], I["rope_rows"].rearrange("(t p) n -> p t n", p=P)),
                             (ws[:], I["w_s"][0].rearrange("g p q -> p g q")), (b_rows[:], I["b_s"][0]),
                             (g_gm[:], I["g_sgu"].to_broadcast((P, D)))):
                pool.dma_start(dst, src).then_inc(consts, 16)
            pool.wait_ge(kv_hat, TT)
            pool.dma_start(O["new_ckv"][0, 0], ckv[:, 0, :]).then_inc(ctx_out, 16)
            pool.wait_ge(rot, 1)
            pool.dma_start(O["new_krope"][0, 0], kr[:, 0, :]).then_inc(ctx_out, 16)
            pool.wait_ge(ctx_out, 32)

        @block.scalar
        def _(act):
            for t in range(TT):
                if t:
                    act.wait_ge(sq, 2 * t)
                act.activation(square[:, 0:Q_LORA], M.qa[:, t, :], ACT.Square, accum_out=st[:, 0, t:t + 1]).then_inc(sq, 1)
                act.activation(square[:, Q_LORA:Q_LORA + KV_LORA], M.kvr[:, t, 0:KV_LORA], ACT.Square,
                               accum_out=st[:, 0, TT + t:TT + t + 1]).then_inc(sq, 1)
            act.wait_ge(var, 2)
            act.activation(st[:, 2, :], st[:, 1, :], ACT.Sqrt).then_inc(std, 1)
            for t in range(TT):
                act.wait_ge(q_tr, t + 1)
                act.activation(M.qaT_hi[:, :, bass.ts(t, P)], ps[t % 2][:].rearrange("p (j n) -> p j n", j=KG),
                               ACT.Copy).then_inc(q_hi, 1)
            for t in range(KEYT):
                act.wait_ge(kv_tr, t + 1)
                act.activation(M.ckvT[:, :, bass.ts(t, P)], ps[2 + t % 2][:, 0:2 * P].rearrange("p (j n) -> p j n", j=2),
                               ACT.Copy).then_inc(kv_f, 1)
                act.activation(M.ckvT_hi[:, :, bass.ts(t, P)], ps[2 + t % 2][:, 0:2 * P].rearrange("p (j n) -> p j n", j=2),
                               ACT.Copy).then_inc(kv_hi, 1)
            for b, (k0, k1) in enumerate(((0, 4 * P), (4 * P, N_KEY))):
                act.wait_ge(kr_tr, b + 1)
                act.activation(M.krT_hi[:, k0:k1], ps[4 + b][0:D_ROPE, 0:k1 - k0], ACT.Copy).then_inc(kr_hi, 1)
            for b in range(2):
                act.wait_ge(ws_tr, b + 1)
                act.activation(wsT[:, 4 * b:4 * b + 4, :], ps[6 + b][:].rearrange("p (j n) -> p j n", j=4), ACT.Copy).then_inc(ws_ev, 1)

            def norm(t):
                act.wait_ge(acts_in[t % 2], 32 * (t // 2 + 1))
                if t:
                    act.wait_ge(g_sq, t)
                act.activation(square[:], gv[t % 2][:], ACT.Square, accum_out=gst[:, 0, t:t + 1]).then_inc(g_sq, 1)
                act.wait_ge(g_var, t + 1)
                act.activation(gst[:, 2, t:t + 1], gst[:, 1, t:t + 1], ACT.Sqrt).then_inc(g_std, 1)

            norm(0)
            for t in range(TT):
                if t + 1 < TT:
                    norm(t + 1)
                if t >= 2:
                    act.wait_ge(g_out[t % 2], 16 * (t // 2))
                for q in range(4):
                    act.wait_ge(g_tr, 4 * t + q + 1)
                    act.activation(turned[t % 2][:, 4 * q:4 * q + 4, :], ps[q][:].rearrange("p (j n) -> p j n", j=4),
                                   ACT.Copy).then_inc(g_ev, 1)

        @block.vector
        def _(dve):
            dve.wait_ge(sq, 2 * TT)
            dve.tensor_scalar(st[:, 1, 0:TT], st[:, 0, 0:TT], 1.0 / Q_LORA, EPS, ALU.mult, ALU.add).then_inc(var, 1)
            dve.tensor_scalar(st[:, 1, TT:], st[:, 0, TT:], 1.0 / KV_LORA, EPS, ALU.mult, ALU.add).then_inc(var, 1)
            dve.wait_ge(std, 1)
            dve.reciprocal(st[:, 3, :], st[:, 2, :]).then_inc(inv, 1)
            dve.wait_ge(inv, 1)
            dve.wait_ge(consts, 16 * N_CONST)
            for t in range(TT):
                dve.scalar_tensor_tensor(M.qa[:, t, :], M.qa[:, t, :], st[:, 3, t:t + 1], g_q[:], ALU.mult, ALU.mult).then_inc(q_hat, 1)
                dve.scalar_tensor_tensor(ckv[:, t, :], M.kvr[:, t, 0:KV_LORA], st[:, 3, TT + t:TT + t + 1], g_kv[:],
                                         ALU.mult, ALU.mult).then_inc(kv_hat, 1)
            raw = M.kvr[:, :, KV_LORA:KVR]
            dve.tensor_tensor(kr_cos[:], raw, table[:, :, 0:D_ROPE], ALU.mult).then_inc(rot_part, 1)
            for t in range(TT):
                for h in range(2):
                    one = lambda ap: ap[:, t, :].rearrange("p (a h f) -> p a h f", a=2, h=2)
                    dve.tensor_tensor(one(kr_sin)[:, :, h, :], one(raw)[:, :, 1 - h, :], one(table[:, :, D_ROPE:])[:, :, h, :],
                                      ALU.mult).then_inc(rot_part, 1)
            dve.wait_ge(rot_part, 1 + 2 * TT)
            dve.tensor_tensor(kr[:, 0:TT, :], kr_cos[:], kr_sin[:], ALU.add).then_inc(rot, 1)
            for t in range(TT):
                dve.wait_ge(q_hi, t + 1)
                dve.tensor_tensor(M.qaT_lo[:, :, bass.ts(t, P)], ps[t % 2][:].rearrange("p (j n) -> p j n", j=KG),
                                  M.qaT_hi[:, :, bass.ts(t, P)].bitcast(F32), ALU.subtract).then_inc(q_lo, 1)
            for t in range(KEYT):
                dve.wait_ge(kv_hi, t + 1)
                dve.tensor_tensor(M.ckvT_lo[:, :, bass.ts(t, P)], ps[2 + t % 2][:, 0:2 * P].rearrange("p (j n) -> p j n", j=2),
                                  M.ckvT_hi[:, :, bass.ts(t, P)].bitcast(F32), ALU.subtract).then_inc(kv_lo, 1)
            for b, (k0, k1) in enumerate(((0, 4 * P), (4 * P, N_KEY))):
                dve.wait_ge(kr_hi, b + 1)
                dve.tensor_tensor(M.krT_lo[:, k0:k1], ps[4 + b][0:D_ROPE, 0:k1 - k0], M.krT_hi[:, k0:k1].bitcast(F32),
                                  ALU.subtract).then_inc(kr_lo, 1)
            dve.wait_ge(ws_tr, 3)
            dve.tensor_copy(b_col[:], ps[5][:, 4 * P - GROUPS:4 * P]).then_inc(ws_ev, 1)

            def norm(t):
                dve.wait_ge(g_sq, t + 1)
                dve.tensor_scalar(gst[:, 1, t:t + 1], gst[:, 0, t:t + 1], 1.0 / D, EPS, ALU.mult, ALU.add).then_inc(g_var, 1)
                dve.wait_ge(g_std, t + 1)
                dve.reciprocal(gst[:, 3, t:t + 1], gst[:, 2, t:t + 1]).then_inc(g_inv, 1)
                dve.wait_ge(g_inv, t + 1)
                dve.scalar_tensor_tensor(gv[t % 2][:], gv[t % 2][:], gst[:, 3, t:t + 1], g_gm[:], ALU.mult, ALU.mult).then_inc(g_hat, 1)

            norm(0)
            dve.wait_ge(ws_ev, 3)
            for t in range(TT):
                if t + 1 < TT:
                    norm(t + 1)
                if t:
                    dve.wait_ge(g_tr, 4 * t)
                dve.wait_ge(g_mm, t + 1)
                for g in range(GROUPS):
                    c = slice(g * GC, (g + 1) * GC)
                    ins = dve.scalar_tensor_tensor(mixed[:, c], ps[4 + g // 2][:, GC * (g % 2):GC * (g % 2) + GC],
                                                   b_col[:, g:g + 1], gu[t % 2][:, c], ALU.add, ALU.mult)
                ins.then_inc(g_mix, 1)

        @block.tensor
        def _(pe):
            for t in range(TT):
                pe.wait_ge(q_hat, t + 1)
                if t >= 2:
                    pe.wait_ge(q_lo, t - 1)
                for j in range(KG):
                    ins = pe.transpose(ps[t % 2][:, bass.ts(j, P)], M.qa[:, t, bass.ts(j, P)], M.ident[:])
                ins.then_inc(q_tr, 1)
            pe.wait_ge(consts, 16 * N_CONST)
            pe.wait_ge(kv_hat, TT)
            for t in range(KEYT):
                if t >= 2:
                    pe.wait_ge(kv_f, t - 1)
                    pe.wait_ge(kv_lo, t - 1)
                for j in range(2):
                    ins = pe.transpose(ps[2 + t % 2][:, bass.ts(j, P)], ckv[:, t, bass.ts(j, P)], M.ident[:])
                ins.then_inc(kv_tr, 1)
            pe.wait_ge(rot, 1)
            for b, tiles in enumerate((range(0, 4), range(4, KEYT))):
                for t in tiles:
                    ins = pe.transpose(ps[4 + b][0:D_ROPE, bass.ts(t - 4 * b, P)], kr[:, t, :], M.ident[:])
                ins.then_inc(kr_tr, 1)
            for b in range(2):
                for j in range(4):
                    ins = pe.transpose(ps[6 + b][:, bass.ts(j, P)], ws[:, 4 * b + j, :], M.ident[:])
                ins.then_inc(ws_tr, 1)
            pe.wait_ge(kr_lo, 2)
            pe.transpose(ps[5][:, 4 * P - GROUPS:4 * P], b_rows[:], M.ident[0:GROUPS, 0:GROUPS]).then_inc(ws_tr, 1)
            pe.wait_ge(ws_ev, 3)
            pe.wait_ge(q_lo, TT)
            pe.wait_ge(kv_lo, KEYT)
            for t in range(TT):
                pe.wait_ge(g_hat, t + 1)
                if t:
                    pe.wait_ge(g_mix, t)
                for g in range(GROUPS):
                    ins = pe.matmul(ps[4 + g // 2][:, GC * (g % 2):GC * (g % 2) + GC], wsT[:, g, :],
                                    gv[t % 2][:, g * GC:(g + 1) * GC], start=True, stop=True)
                ins.then_inc(g_mm, 1)
                pe.wait_ge(g_mix, t + 1)
                for q in range(4):
                    if t:
                        pe.wait_ge(g_ev, 4 * (t - 1) + q + 1)
                    for j in range(4):
                        ins = pe.transpose(ps[q][:, bass.ts(j, P)], mixed[:, bass.ts(4 * q + j, P)], M.ident[:])
                    ins.then_inc(g_tr, 1)


HW_Q, HW_K, HW_V = KG * D_Q, 2 * D_NOPE, 2 * D_V


def phase_heads(nc, M, I, W):
    m = Map(nc, W.at)
    raw = m.new("hw_raw", [P, 2, HW_Q + HW_K + HW_V], F32)
    part_hi, part_lo = (m.new(f"hw_{h}", [P, 2, KG * 2 * P + HW_K], F32R) for h in ("hi", "lo"))
    table = m.new("rope_cols_sb", [P, N_TOK], F32)
    prob = [m.new(f"prob{b}", [P, LAT_KEYS], F32) for b in range(2)]
    o_sb = [m.new(f"oT{b}", [P, N_TOK], F32) for b in range(2)]
    rot = [m.new(f"rot{b}", [D_ROPE, N_TOK], F32) for b in range(2)]
    assert m.at <= M.phase_at
    m = Map(nc, M.heads_at)
    two = lambda name, shape: [[m.new(f"{name}_{h}{b}", shape, F32R) for h in ("hi", "lo")] for b in range(2)]
    qn, qr, kn, v = two("qn", [P, N_TOK]), two("qr", [D_ROPE, N_TOK]), two("kn", [P, N_KEY]), two("v", [P, KEYT, D_V])
    pT = [m.new(f"pT_{h}", [P, LAT_KEYS // P, N_LAT], F32R) for h in ("hi", "lo")]
    pTc = [m.new(f"pTc_{h}", [P, N_CTX], F32R) for h in ("hi", "lo")]
    red = m.new("softmax_cols", [P, 4, 2], F32)

    with ExitStack() as ctx:
        sem = phase_semaphores(ctx, nc)
        pair = [ctx.enter_context(nc.psum_tensor(f"h_ps{b}", [P, 2, NC], F32)) for b in range(4)]
        raw_in = [sem("hw_in0"), sem("hw_in1")]
        w_hi, w_lo = sem("hw_hi_done"), sem("hw_lo_done")
        pq, pr, pk, pv = (sem(f"proj_{n}") for n in ("q", "rope", "k", "v"))
        rot_part, rot_sum, e_hi, e_lo = sem("rot_part"), sem("rot_sum"), sem("part_hi"), sem("part_lo")
        s_done, mx_ok, neg_ok, exp_ok, inv_ok, p_ok, t_done, pt_hi, pt_lo, o_done, o_ev = (
            sem(n) for n in ("s_done", "mx_ok", "neg_ok", "exp_ok", "inv_ok", "p_ok", "t_done", "pt_hi", "pt_lo", "o_done", "o_ev"))
        o_out, tab_in = [sem("o_out0"), sem("o_out1")], sem("tab_in")
        block = ctx.enter_context(nc.Block())
        TILES = TT
        W_QB = I["w_qb"][0].rearrange("(j p) n -> p j n", p=P)
        W_UK, W_UV = (I[n][0].rearrange("(j p) h d -> p j (h d)", p=P) for n in ("w_uk", "w_uv"))

        def q_part(t, b):
            return t[:, b, 0:KG * 2 * P].rearrange("p (j n) -> p j n", j=KG)

        def k_part(t, b):
            return t[:, b, KG * 2 * P:]

        def raw_q(b):
            return raw[:, b, 0:HW_Q].rearrange("p (j n) -> p j n", j=KG)

        def swap(ap):
            return ap.rearrange("p j (a h f) -> p j a h f", a=2, h=2)

        def load_head(sp, n, b):
            sp.wait_ge(w_lo, n + 1)
            sp.wait_ge(pv, n + 1)
            for dst, src in ((raw_q(b), W_QB[:, :, bass.ds(n * D_Q, D_Q)]),
                             (raw[:, b, HW_Q:HW_Q + HW_K].rearrange("p (j n) -> p j n", j=2), W_UK[:, :, bass.ds(n * D_NOPE, D_NOPE)]),
                             (raw[:, b, HW_Q + HW_K:].rearrange("p (j n) -> p j n", j=2), W_UV[:, :, bass.ds(n * D_V, D_V)])):
                sp.dma_start(dst, src).then_inc(raw_in[b], 16)

        def store_head(sp, a, b, k):
            sp.wait_ge(o_ev, a + 2)
            sp.dma_start(M.oaT[bass.ds(a * D_V, D_V), :], o_sb[b][:]).then_inc(o_out[b], 16)

        @block.sync
        def _(sp):
            sp.sem_inc(o_out[0], 16)
            sp.sem_inc(o_out[1], 16)
            sp.dma_start(table[:], I["rope_cols"]).then_inc(tab_in, 16)
            for n in range(2):
                load_head(sp, n, n)
            with sp.Fori(0, HEADS // 2 - 1) as i:
                for b in range(2):
                    load_head(sp, 2 * i + b + 2, b)
                    store_head(sp, 2 * i + b, b, i)
            for b in range(2):
                store_head(sp, HEADS - 2 + b, b, HEADS // 2 - 1)
                sp.wait_ge(o_out[b], 16 * (HEADS // 2 + 1))

        @block.scalar
        def _(act):
            def weights(n, b, k):
                act.wait_ge(raw_in[b], 48 * k + 48)
                act.wait_ge(pk, n + 1)
                q = q_part(part_hi, b)
                act.activation(q[:, :, 0:D_Q], raw_q(b), ACT.Copy)
                for h in range(2):
                    for x in range(2):
                        act.activation(swap(q[:, :, D_Q:])[:, :, x, h, :], swap(raw_q(b)[:, :, D_NOPE:])[:, :, x, 1 - h, :], ACT.Copy)
                act.activation(k_part(part_hi, b), raw[:, b, HW_Q:HW_Q + HW_K], ACT.Copy).then_inc(w_hi, 1)

            def evac_qn(n, b):
                act.wait_ge(pq, n + 1)
                act.activation(qn[b][0][:].rearrange("p (c n) -> p c n", c=2), pair[0][:, :, 0:N_TOK // 2], ACT.Copy).then_inc(e_hi, 1)

            def evac_qr(n, b):
                act.wait_ge(rot_sum, n + 1)
                act.activation(qr[b][0][:], rot[0][:], ACT.Copy).then_inc(e_hi, 1)

            def evac_kn(n, b):
                act.wait_ge(pk, n + 3)
                act.activation(kn[b][0][:].rearrange("p (c n) -> p c n", c=2), pair[0][:, :, 0:N_KEY // 2], ACT.Copy).then_inc(e_hi, 1)

            def evac_v(n, b):
                act.wait_ge(pv, n + 3)
                act.activation(v[b][0][:, 0:4, :], pair[1][:, 0, :].rearrange("p (t d) -> p t d", t=4), ACT.Copy)
                act.activation(v[b][0][:, 4:KEYT, :], pair[1][:, 1, 0:(KEYT - 4) * P].rearrange("p (t d) -> p t d", d=P), ACT.Copy).then_inc(e_hi, 1)

            def exp(a, u):
                c = u % 2
                act.wait_ge(neg_ok, TILES * a + u + 1)
                width = N_CTX if u == 0 else LAT_KEYS
                src = pair[2 + c][:, 0, 0:P] if u == 0 else pair[2 + c][:, :, 0:LAT_KEYS // 2]
                dst = prob[c][:, 0:width] if u == 0 else prob[c][:].rearrange("p (c n) -> p c n", c=2)
                act.activation(dst, src, ACT.Exp, bias=red[:, 1, c:c + 1], scale=SM_SCALE, accum_out=red[:, 2, c:c + 1]).then_inc(exp_ok, 1)

            def turn_hi(a, u):
                c = u % 2
                act.wait_ge(t_done, TILES * a + u + 1)
                if u == 0:
                    act.wait_ge(o_done, 2 * a + 2)
                    act.activation(pTc[0][:], pair[2 + c][:, 0, 0:P], ACT.Copy).then_inc(pt_hi, 1)
                else:
                    act.activation(pT[0][:, :, bass.ts(u - 1, P)].rearrange("p (c k) q -> p c k q", c=2),
                                   pair[2 + c][:, :, 0:LAT_KEYS // 2].rearrange("p c (k q) -> p c k q", q=P), ACT.Copy).then_inc(pt_hi, 1)

            def step(a, b, k, proj=True, ahead=True):
                n, nb = a + 1, 1 - b
                exp(a, 0)
                exp(a, 1)
                if proj:
                    evac_qn(n, nb)
                turn_hi(a, 0)
                if proj:
                    evac_qr(n, nb)
                exp(a, 2)
                turn_hi(a, 1)
                if proj:
                    evac_kn(n, nb)
                exp(a, 3)
                turn_hi(a, 2)
                exp(a, 4)
                turn_hi(a, 3)
                if proj:
                    evac_v(n, nb)
                if ahead:
                    weights(a + 2, b, k + 1)
                turn_hi(a, 4)
                act.wait_ge(o_out[b], 16 * k + 16)
                act.wait_ge(o_done, 2 * a + 4)
                act.activation(o_sb[b][:, 0:N_CTX], pair[0][:, 1, 0:N_CTX], ACT.Copy)
                act.activation(o_sb[b][:, N_CTX:], pair[0][:, 0, :], ACT.Copy).then_inc(o_ev, 1)

            weights(0, 0, 0)
            weights(1, 1, 0)
            evac_qn(0, 0)
            evac_qr(0, 0)
            evac_kn(0, 0)
            evac_v(0, 0)
            with act.Fori(0, HEADS // 2 - 1) as i:
                for b in range(2):
                    step(2 * i + b, b, i)
            step(HEADS - 2, 0, HEADS // 2 - 1, ahead=False)
            step(HEADS - 1, 1, HEADS // 2 - 1, proj=False, ahead=False)

        @block.vector
        def _(dve):
            dve.sem_inc(w_lo, 2)
            dve.sem_inc(pt_lo, TILES)
            lo = lambda out, src, hi: dve.tensor_tensor(out, src, hi.bitcast(F32), ALU.subtract)

            def weights(n, b):
                dve.wait_ge(w_hi, n + 1)
                q, ql = q_part(part_hi, b), q_part(part_lo, b)
                lo(ql[:, :, 0:D_Q], raw_q(b), q[:, :, 0:D_Q])
                for h in range(2):
                    for x in range(2):
                        lo(swap(ql[:, :, D_Q:])[:, :, x, h, :], swap(raw_q(b)[:, :, D_NOPE:])[:, :, x, 1 - h, :],
                           swap(q[:, :, D_Q:])[:, :, x, h, :])
                lo(k_part(part_lo, b), raw[:, b, HW_Q:HW_Q + HW_K], k_part(part_hi, b)).then_inc(w_lo, 1)

            def evac_qn(n, b):
                dve.wait_ge(e_hi, 4 * n + 1)
                lo(qn[b][1][:].rearrange("p (c n) -> p c n", c=2), pair[0][:, :, 0:N_TOK // 2],
                   qn[b][0][:].rearrange("p (c n) -> p c n", c=2)).then_inc(e_lo, 1)

            def rotate(n):
                dve.wait_ge(pr, n + 1)
                dve.wait_ge(e_lo, 4 * n + 1)
                for c, (x, y) in enumerate(((0, D_ROPE), (D_ROPE, P))):
                    dve.tensor_tensor(rot[c][:].rearrange("p (c n) -> p c n", c=2), pair[1][x:y, :, 0:N_TOK // 2],
                                      table[x:y, :].rearrange("p (c n) -> p c n", c=2), ALU.mult).then_inc(rot_part, 1)
                dve.wait_ge(rot_part, 2 * n + 2)
                dve.tensor_tensor(rot[0][:], rot[0][:], rot[1][:], ALU.add).then_inc(rot_sum, 1)

            def evac_qr(n, b):
                dve.wait_ge(e_hi, 4 * n + 2)
                lo(qr[b][1][:], rot[0][:], qr[b][0][:]).then_inc(e_lo, 1)

            def evac_kn(n, b):
                dve.wait_ge(e_hi, 4 * n + 3)
                lo(kn[b][1][:].rearrange("p (c n) -> p c n", c=2), pair[0][:, :, 0:N_KEY // 2],
                   kn[b][0][:].rearrange("p (c n) -> p c n", c=2)).then_inc(e_lo, 1)

            def evac_v(n, b):
                dve.wait_ge(e_hi, 4 * n + 4)
                lo(v[b][1][:, 0:4, :], pair[1][:, 0, :].rearrange("p (t d) -> p t d", t=4), v[b][0][:, 0:4, :])
                lo(v[b][1][:, 4:KEYT, :], pair[1][:, 1, 0:(KEYT - 4) * P].rearrange("p (t d) -> p t d", d=P),
                   v[b][0][:, 4:KEYT, :]).then_inc(e_lo, 1)

            def top(a, u):
                c, n = u % 2, TILES * a + u
                dve.wait_ge(s_done, n + 1)
                src = pair[2 + c][:, 0, 0:P] if u == 0 else pair[2 + c][:, :, 0:LAT_KEYS // 2]
                dve.tensor_reduce(red[:, 0, c:c + 1], src, AX.X if u == 0 else AX.XY, ALU.max).then_inc(mx_ok, 1)
                dve.wait_ge(mx_ok, n + 1)
                dve.tensor_scalar(red[:, 1, c:c + 1], red[:, 0, c:c + 1], -SM_SCALE, None, ALU.mult).then_inc(neg_ok, 1)

            def divide(a, u):
                c, n = u % 2, TILES * a + u
                dve.wait_ge(exp_ok, n + 1)
                dve.reciprocal(red[:, 3, c:c + 1], red[:, 2, c:c + 1]).then_inc(inv_ok, 1)
                dve.wait_ge(inv_ok, n + 1)
                width = N_CTX if u == 0 else LAT_KEYS
                dve.tensor_scalar(prob[c][:, 0:width], prob[c][:, 0:width], red[:, 3, c:c + 1], None, ALU.mult).then_inc(p_ok, 1)

            def turn_lo(a, u):
                c = u % 2
                dve.wait_ge(pt_hi, TILES * a + u + 1)
                if u == 0:
                    lo(pTc[1][:], pair[2 + c][:, 0, 0:P], pTc[0][:]).then_inc(pt_lo, 1)
                else:
                    part = lambda h: pT[h][:, :, bass.ts(u - 1, P)].rearrange("p (c k) q -> p c k q", c=2)
                    lo(part(1), pair[2 + c][:, :, 0:LAT_KEYS // 2].rearrange("p c (k q) -> p c k q", q=P), part(0)).then_inc(pt_lo, 1)

            def step(a, b, proj=True, ahead=True):
                n, nb = a + 1, 1 - b
                top(a, 0)
                top(a, 1)
                divide(a, 0)
                divide(a, 1)
                if proj:
                    evac_qn(n, nb)
                turn_lo(a, 0)
                if proj:
                    rotate(n)
                top(a, 2)
                if proj:
                    evac_qr(n, nb)
                turn_lo(a, 1)
                divide(a, 2)
                top(a, 3)
                if proj:
                    evac_kn(n, nb)
                turn_lo(a, 2)
                divide(a, 3)
                top(a, 4)
                turn_lo(a, 3)
                divide(a, 4)
                if proj:
                    evac_v(n, nb)
                if ahead:
                    weights(a + 2, b)
                turn_lo(a, 4)

            weights(0, 0)
            weights(1, 1)
            dve.wait_ge(tab_in, 16)
            evac_qn(0, 0)
            rotate(0)
            evac_qr(0, 0)
            evac_kn(0, 0)
            evac_v(0, 0)
            with dve.Fori(0, HEADS // 2 - 1) as i:
                for b in range(2):
                    step(2 * i + b, b)
            step(HEADS - 2, 0, ahead=False)
            step(HEADS - 1, 1, proj=False, ahead=False)

        @block.tensor
        def _(pe):
            pe.sem_inc(pk, 2)
            pe.sem_inc(pv, 2)
            pe.sem_inc(o_done, 2)
            pe.sem_inc(o_ev, 1)

            def proj_q(n, b, which):
                if which == 0:
                    pe.wait_ge(w_lo, n + 3)
                c0 = P * which
                for half in range(2):
                    for k in range(KG):
                        cols = slice(half * N_TOK // 2, (half + 1) * N_TOK // 2)
                        ins = product(pe, pair[which][:, half, 0:N_TOK // 2], q_part(part_hi, b)[:, k, c0:c0 + P],
                                      q_part(part_lo, b)[:, k, c0:c0 + P], M.qaT_hi[:, k, cols], M.qaT_lo[:, k, cols],
                                      k == 0, k == KG - 1)
                ins.then_inc(pr if which else pq, 1)

            def proj_k(n, b):
                pe.wait_ge(e_lo, 4 * n + 1)
                for half in range(2):
                    for k in range(2):
                        cols = slice(half * N_KEY // 2, (half + 1) * N_KEY // 2)
                        ins = product(pe, pair[0][:, half, 0:N_KEY // 2], k_part(part_hi, b)[:, bass.ts(k, P)],
                                      k_part(part_lo, b)[:, bass.ts(k, P)], M.ckvT_hi[:, k, cols], M.ckvT_lo[:, k, cols],
                                      k == 0, k == 1)
                ins.then_inc(pk, 1)

            def proj_v(n, b, tiles):
                if tiles[0] == 0:
                    pe.wait_ge(rot_sum, n + 1)
                for t in tiles:
                    for k in range(2):
                        ins = pe.matmul(pair[1][:, t // 4, bass.ts(t % 4, P)], M.ckvT[:, k, bass.ts(t, P)],
                                        raw[:, b, HW_Q + HW_K + k * P:HW_Q + HW_K + (k + 1) * P], start=(k == 0), stop=(k == 1))
                if tiles[-1] == KEYT - 1:
                    ins.then_inc(pv, 1)

            def scores(a, b, u):
                c = u % 2
                pe.wait_ge(pt_lo, TILES * a + TILES if u == 0 else TILES * a + TILES - 1 if u == 1 else TILES * a + TILES + u - 1)
                if u == 0:
                    pe.wait_ge(e_lo, 4 * a + 3)
                rows = bass.ts(u, P)
                for k0, k1, out in (((0, P, pair[2 + c][:, 0, 0:P]),) if u == 0 else
                                    ((N_CTX, N_CTX + LAT_KEYS // 2, pair[2 + c][:, 0, 0:LAT_KEYS // 2]),
                                     (N_CTX + LAT_KEYS // 2, N_KEY, pair[2 + c][:, 1, 0:LAT_KEYS // 2]))):
                    product(pe, out, qn[b][0][:, rows], qn[b][1][:, rows], kn[b][0][:, k0:k1], kn[b][1][:, k0:k1], True, False)
                    ins = product(pe, out, qr[b][0][:, rows], qr[b][1][:, rows], M.krT_hi[:, k0:k1], M.krT_lo[:, k0:k1], False, True)
                ins.then_inc(s_done, 1)

            def turn(a, u):
                c = u % 2
                pe.wait_ge(p_ok, TILES * a + u + 1)
                for k in range(1 if u == 0 else LAT_KEYS // P):
                    ins = pe.transpose(pair[2 + c][:, k // 3, bass.ts(k % 3, P)], prob[c][:, bass.ts(k, P)], M.ident[:])
                ins.then_inc(t_done, 1)

            def mix(a, b, proj):
                if proj:
                    pe.wait_ge(e_lo, 4 * a + 7)
                pe.wait_ge(pt_lo, TILES * a + 1 + TILES)
                product(pe, pair[0][:, 1, 0:N_CTX], v[b][0][:, 0, :], v[b][1][:, 0, :], pTc[0][:], pTc[1][:], True, True).then_inc(o_done, 1)
                pe.wait_ge(pt_lo, TILES * (a + 2))
                for k in range(LAT_KEYS // P):
                    ins = product(pe, pair[0][:, 0, :], v[b][0][:, k + 1, :], v[b][1][:, k + 1, :], pT[0][:, k, :], pT[1][:, k, :],
                                  k == 0, k == LAT_KEYS // P - 1)
                ins.then_inc(o_done, 1)

            def step(a, b, proj=True):
                n, nb = a + 1, 1 - b
                scores(a, b, 0)
                scores(a, b, 1)
                if proj:
                    pe.wait_ge(o_ev, a + 1)
                    proj_q(n, nb, 0)
                turn(a, 0)
                if proj:
                    pe.wait_ge(e_lo, 4 * a + 4)
                    proj_q(n, nb, 1)
                scores(a, b, 2)
                turn(a, 1)
                if proj:
                    proj_k(n, nb)
                scores(a, b, 3)
                turn(a, 2)
                if proj:
                    proj_v(n, nb, range(0, 4))
                scores(a, b, 4)
                turn(a, 3)
                if proj:
                    proj_v(n, nb, range(4, KEYT))
                turn(a, 4)
                mix(a, b, proj)

            proj_q(0, 0, 0)
            proj_q(0, 0, 1)
            proj_k(0, 0)
            proj_v(0, 0, range(0, 4))
            proj_v(0, 0, range(4, KEYT))
            with pe.Fori(0, HEADS // 2 - 1) as i:
                for b in range(2):
                    step(2 * i + b, b)
            step(HEADS - 2, 0)
            step(HEADS - 1, 1, proj=False)


def phase_project(nc, M, I, W, kind):
    m = Map(nc, M.phase_at)
    x_hi, x_lo = (m.new(f"{kind}_xT_{h}", [P, KT, N_TOK], F32R) for h in ("hi", "lo"))
    x_raw = m.new(f"{kind}_xT_raw", [P, 2, KG, N_TOK], F32)
    side = m.new(f"{kind}_side", [P, TT, NC], F32)
    more = m.new(f"{kind}_more", [P, TT, NC], F32)
    if kind == "gm":
        turned = m.new("gm_back", [P, 2, KG, P], F32)
    if kind == "out":
        gate = m.new("gate1", [P, 2, NC], F32)
    N_CH = D // NC
    source = {"mla": M.oaT, "gm": M.obT, "out": M.mT}[kind]
    weight = {"mla": "w_o_mla", "gm": "w_o_gm", "out": "w_out"}[kind]
    XT = source.rearrange("(g j p) n -> g p j n", g=KG, j=KG)
    WT = I[weight].rearrange("l (g j p) n -> (l g) p j n", g=KG, j=KG)
    N_SIDE = {"mla": TT, "gm": 2 * TT, "out": TT + 2}[kind]

    with ExitStack() as ctx:
        new = phase_semaphores(ctx, nc)
        sem = lambda n: new(f"proj_{kind}_{n}")
        ps = [ctx.enter_context(nc.psum_tensor(f"{kind}_ps{b}", [P, NC], F32)) for b in range(8)]
        d = Stream(sem, "w", 4, 2)
        x_in, x_h, x_l = [sem("x_in0"), sem("x_in1")], sem("x_hi"), sem("x_lo")
        acc_ready, acc_free, passed = sem("acc_ready"), sem("acc_free"), sem("passed")
        side_in, stored = M.pool_sem(f"{kind}_side_in"), M.pool_sem(f"{kind}_stored")
        prod, res, tr, tr_ev, back_free = sem("prod"), sem("res"), sem("tr"), sem("tr_ev"), sem("back_free")
        block = ctx.enter_context(nc.Block())
        stage = lambda g: W.stage[:, g, :]

        @block.sync
        def _(sp):
            def weights(n, i, g):
                load_piece(sp, d, n, g, stage(g).rearrange("p (j n) -> p j n", j=KG), WT[g][:, :, bass.ds(i * NC, NC)])
            for g in range(KG):
                if g >= 2:
                    sp.wait_ge(x_l, g - 1)
                sp.dma_start(x_raw[:, g % 2], XT[g]).then_inc(x_in[g % 2], 16)
                weights(g, 0, g)
            with sp.Fori(1, N_CH) as i:
                for g in range(KG):
                    weights(KG * i + g, i, g)

        @block.gpsimd
        def _(pool):
            pool.sem_inc(back_free, 2)
            pool.sem_inc(tr_ev, 2)
            tile = lambda ap, t, i, c0=0: ap[bass.ts(t, P), bass.ds(i * NC + c0, NC)]
            with pool.Fori(0, N_CH) as i:
                for t in range(TT):
                    if kind == "out":
                        src = (I["x_prompt"][0] if t == 0 else I["x_sample"][0, bass.ts(t - 1, P), :])[:, bass.ds(i * NC, NC)]
                    else:
                        src = tile(M.acts, t, i, 2 * D if kind == "mla" else 3 * D)
                    pool.dma_start(side[:, t, :], src).then_inc(side_in, 16)
                    if kind == "gm":
                        pool.dma_start(more[:, t, :], tile(M.ma, t, i)).then_inc(side_in, 16)
                if kind == "out":
                    for r in range(2):
                        pool.dma_start(gate[:, r, :], M.mod[r:r + 1, bass.ds(i * NC + 2 * D, NC)].to_broadcast((P, NC))).then_inc(side_in, 16)
                for t in range(TT):
                    if kind == "gm":
                        pool_wait(pool, tr_ev, TT * i + t + 3, passed)
                        pool.dma_start(M.mT.rearrange("(j p) n -> p j n", p=P)[:, bass.ds(i * KG, KG), bass.ts(t, P)],
                                       turned[:, t % 2]).then_inc(stored, 16)
                        pool_wait(pool, stored, 16 * TT * i + 16 * t + 16, back_free)
                    else:
                        pool_wait(pool, res, TT * i + t + 1, passed)
                        pool.dma_start(tile(M.ma if kind == "mla" else M.xn, t, i), side[:, t, :]).then_inc(stored, 16)
                pool_wait(pool, stored, 16 * TT * i + 16 * TT, passed)

        @block.scalar
        def _(act):
            def weights(n, i, g):
                piece_hi(act, d, n, g, i + 1, W.hi[:, g % 2, :], stage(g))

            def back(i):
                for t in range(TT):
                    act.wait_ge(tr, TT * i + t + 1)
                    act.wait_ge(back_free, TT * i + t + 1)
                    act.activation(turned[:, t % 2], ps[5 + t % 2][:].rearrange("p (j n) -> p j n", j=KG), ACT.Copy).then_inc(tr_ev, 1)

            for g in range(KG):
                act.wait_ge(x_in[g % 2], 16 * (g // 2 + 1))
                act.activation(x_hi[:, KG * g:KG * g + KG, :], x_raw[:, g % 2], ACT.Copy).then_inc(x_h, 1)
                weights(g, 0, g)
            with act.Fori(1, N_CH) as i:
                for g in range(KG):
                    weights(KG * i + g, i, g)
                    if g == 1 and kind == "gm":
                        back(i - 1)
            if kind == "gm":
                back(N_CH - 1)

        @block.vector
        def _(dve):
            dve.sem_inc(d.split, d.n_stage)
            def weights(n, g):
                piece_lo(dve, d, n, W.lo[:, g % 2, :], stage(g), W.hi[:, g % 2, :])

            def combine(i):
                dve.wait_ge(side_in, 16 * N_SIDE * i + 16 * N_SIDE)
                for t in range(TT):
                    wait_acc(dve, d, acc_ready, i, t)
                    if kind == "out":
                        dve.tensor_tensor(more[:, t, :], ps[t][:], gate[:, min(t, 1), :], ALU.mult).then_inc(acc_free, 1)
                        dve.wait_ge(acc_free, TT * i + t + 1)
                        dve.tensor_tensor(side[:, t, :], side[:, t, :], more[:, t, :], ALU.add).then_inc(res, 1)
                    elif kind == "mla":
                        dve.tensor_tensor(side[:, t, :], ps[t][:], side[:, t, :], ALU.mult).then_inc(acc_free, 1)
                        dve.wait_ge(acc_free, TT * i + t + 1)
                        dve.sem_inc(res, 1)
                    else:
                        dve.tensor_tensor(side[:, t, :], ps[t][:], side[:, t, :], ALU.mult).then_inc(acc_free, 1)
                        dve.wait_ge(acc_free, TT * i + t + 1)
                        dve.tensor_tensor(more[:, t, :], side[:, t, :], more[:, t, :], ALU.add).then_inc(res, 1)

            for g in range(KG):
                dve.wait_ge(x_h, g + 1)
                dve.tensor_tensor(x_lo[:, KG * g:KG * g + KG, :], x_raw[:, g % 2], x_hi[:, KG * g:KG * g + KG, :].bitcast(F32),
                                  ALU.subtract).then_inc(x_l, 1)
                weights(g, g)
            with dve.Fori(1, N_CH) as i:
                for g in range(KG):
                    weights(KG * i + g, g)
                    if g == 0:
                        combine(i - 1)
            combine(N_CH - 1)

        @block.tensor
        def _(pe):
            pe.sem_inc(d.used, d.n_w)

            def turn(i):
                for t in range(TT):
                    pe.wait_ge(res, TT * i + t + 1)
                    pe.wait_ge(tr_ev, TT * i + t + 1)
                    for j in range(KG):
                        ins = pe.transpose(ps[5 + t % 2][:, bass.ts(j, P)], more[:, t, bass.ts(j, P)], M.ident[:])
                    ins.then_inc(tr, 1)

            def chunk(i, evacuated):
                for g in range(KG):
                    pe.wait_ge(x_l, g + 1)
                    dense_piece(pe, d, KG * i + g, g, g % 2, W, x_hi, x_lo, ps, acc_ready, acc_free, evacuated)
                    if g == 0 and kind == "gm" and evacuated is not None:
                        turn(i - 1)
            chunk(0, None)
            with pe.Fori(1, N_CH) as i:
                chunk(i, TT * (i - 1))
            if kind == "gm":
                turn(N_CH - 1)


def phase_route(nc, M, I, W):
    m = Map(nc, M.phase_at)
    M.gates = m.new("gates", [SLOTS, EXPERTS], F32)
    M.rows = m.new("rows", [SLOTS, EXPERTS], U32)
    M.route_at = m.at
    xr = [m.new(f"r_x{b}", [P, D], F32) for b in range(2)]
    gain = m.new("r_gain", [P, 2, D], F32)
    shift = m.new("r_shift", [P, 2, D], F32)
    g_row = m.new("r_g", [P, D], F32)
    square = m.new("r_square", [P, D], F32)
    hT = [m.new(f"r_hT{b}", [P, KT, P], F32) for b in range(2)]
    w_r = m.new("w_router_sb", [P, KT, EXPERTS], F32)
    st = m.new("r_stats", [P, 4, TT], F32)
    sm = m.new("r_softmax", [P, 4, TT], F32)
    logits = m.new("r_logits", [P, TT, EXPERTS], F32)
    aff = m.new("r_aff", [P, TT, EXPERTS], F32)
    affT = m.new("r_affT", [EXPERTS, N_TOK], F32)
    val = m.new("r_val", [EXPERTS, SLOTS], F32)
    idx = m.new("r_idx", [EXPERTS, SLOTS], U32)
    idx_f = m.new("r_idx_f", [EXPERTS, SLOTS], F32)

    with ExitStack() as ctx:
        sem = phase_semaphores(ctx, nc)
        ps = [ctx.enter_context(nc.psum_tensor(f"r_ps{b}", [P, NC], F32)) for b in range(8)]
        x_in, h_out = [sem("r_x_in0"), sem("r_x_in1")], [sem("r_h_out0"), sem("r_h_out1")]
        rows_in, w_in, zero, zeroed = sem("r_rows_in"), sem("r_w_in"), sem("r_zero"), M.pool_sem("r_zeroed")
        sq, var, std, inv, gain1, gain_ok, scaled, h_ok, h_tr, h_ev, logit, logit_ok, top, neg, ex, ex_inv, aff_ok, aff_tr, aff_ev = (
            sem(f"r_{n}") for n in ("sq", "var", "std", "inv", "gain1", "gain_ok", "scaled", "h_ok", "h_tr", "h_ev", "logit", "logit_ok", "top", "neg",
                                    "ex", "ex_inv", "aff_ok", "aff_tr", "aff_ev"))
        picked, picks, pick_tr, pick_ok = sem("r_picked"), sem("r_picks"), sem("r_pick_tr"), sem("r_pick_ok")
        block = ctx.enter_context(nc.Block())

        @block.sync
        def _(sp):
            sp.dma_start(xr[0][:], M.xn[bass.ts(0, P), :]).then_inc(x_in[0], 16)
            for r in range(2):
                sp.dma_start(gain[:, r, :], M.mod[r:r + 1, 4 * D:5 * D].to_broadcast((P, D))).then_inc(rows_in, 16)
            sp.dma_start(g_row[:], I["g_ffn"].to_broadcast((P, D))).then_inc(rows_in, 16)
            for r in range(2):
                sp.dma_start(shift[:, r, :], M.mod[r:r + 1, 3 * D:4 * D].to_broadcast((P, D))).then_inc(rows_in, 16)
            sp.dma_start(w_r[:], I["w_router"][0].rearrange("(k p) n -> p k n", p=P)).then_inc(w_in, 16)
            for t in range(TT):
                if t + 1 < TT:
                    if t:
                        sp.wait_ge(h_out[(t + 1) % 2], 16 * ((t + 1) // 2))
                        sp.wait_ge(h_tr, 4 * t)
                    sp.dma_start(xr[(t + 1) % 2][:], M.xn[bass.ts(t + 1, P), :]).then_inc(x_in[(t + 1) % 2], 16)
                sp.wait_ge(h_ok, t + 1)
                sp.dma_start(M.h2[bass.ts(t, P), :], xr[t % 2][:]).then_inc(h_out[t % 2], 16)
            sp.wait_ge(h_out[0], 16 * ((TT + 1) // 2))
            sp.wait_ge(h_out[1], 16 * (TT // 2))

        @block.gpsimd
        def _(pool):
            pool.memset(hT[1][:], 0.0).then_inc(zero, 1)
            pool.wait_ge(zero, 1)
            for t in range(TT):
                pool.dma_start(M.moe[bass.ts(t, P), :], hT[1][:].rearrange("p k n -> p (k n)")).then_inc(zeroed, 16)
            pool.wait_ge(zeroed, 16 * TT)

        @block.scalar
        def _(act):
            def norm(t):
                act.wait_ge(x_in[t % 2], 16 * (t // 2 + 1))
                if t:
                    act.wait_ge(sq, t)
                act.activation(square[:], xr[t % 2][:], ACT.Square, accum_out=st[:, 0, t:t + 1]).then_inc(sq, 1)
                act.wait_ge(var, t + 1)
                act.activation(st[:, 2, t:t + 1], st[:, 1, t:t + 1], ACT.Sqrt).then_inc(std, 1)

            act.wait_ge(zeroed, 16 * TT)
            norm(0)
            for t in range(TT):
                if t + 1 < TT:
                    norm(t + 1)
                for q in range(4):
                    act.wait_ge(h_tr, 4 * t + q + 1)
                    if t >= 2 and q == 0:
                        act.wait_ge(logit, t - 1)
                    act.activation(hT[t % 2][:, 4 * q:4 * q + 4, :], ps[q][:].rearrange("p (j n) -> p j n", j=4), ACT.Copy).then_inc(h_ev, 1)
            for t in range(TT):
                if t == 0:
                    act.wait_ge(neg, 1)
                act.activation(aff[:, t, :], logits[:, t, :], ACT.Exp, bias=sm[:, 1, t:t + 1],
                               accum_out=sm[:, 2, t:t + 1]).then_inc(ex, 1)

        @block.vector
        def _(dve):
            def norm(t):
                dve.wait_ge(sq, t + 1)
                dve.tensor_scalar(st[:, 1, t:t + 1], st[:, 0, t:t + 1], 1.0 / D, EPS, ALU.mult, ALU.add).then_inc(var, 1)
                dve.wait_ge(std, t + 1)
                dve.reciprocal(st[:, 3, t:t + 1], st[:, 2, t:t + 1]).then_inc(inv, 1)
                dve.wait_ge(inv, t + 1)
                if t == 0:
                    dve.wait_ge(rows_in, 80)
                    for r in range(2):
                        dve.scalar_tensor_tensor(gain[:, r, :], gain[:, r, :], 1.0, g_row[:], ALU.add, ALU.mult).then_inc(gain_ok, 1)
                dve.wait_ge(gain_ok, 2)
                dve.scalar_tensor_tensor(xr[t % 2][:], xr[t % 2][:], st[:, 3, t:t + 1], gain[:, min(t, 1), :], ALU.mult, ALU.mult).then_inc(scaled, 1)
                dve.wait_ge(scaled, t + 1)
                dve.tensor_tensor(xr[t % 2][:], xr[t % 2][:], shift[:, min(t, 1), :], ALU.add).then_inc(h_ok, 1)

            for t in range(TT):
                norm(t)
            dve.wait_ge(logit, TT)
            dve.tensor_copy(logits[:].rearrange("p t e -> p (t e)"), ps[4][:, 0:TT * EXPERTS]).then_inc(logit_ok, 1)
            dve.wait_ge(logit_ok, 1)
            dve.tensor_reduce(sm[:, 0, :], logits[:], AX.X, ALU.max).then_inc(top, 1)
            dve.wait_ge(top, 1)
            dve.tensor_scalar(sm[:, 1, :], sm[:, 0, :], -1.0, None, ALU.mult).then_inc(neg, 1)
            for t in range(TT):
                dve.wait_ge(ex, t + 1)
                dve.reciprocal(sm[:, 3, t:t + 1], sm[:, 2, t:t + 1]).then_inc(ex_inv, 1)
                dve.wait_ge(ex_inv, t + 1)
                dve.tensor_scalar(aff[:, t, :], aff[:, t, :], sm[:, 3, t:t + 1], None, ALU.mult).then_inc(aff_ok, 1)
            dve.wait_ge(aff_tr, TT)
            dve.tensor_copy(affT[:, 0:N_LAT], ps[5][0:EXPERTS, :]).then_inc(aff_ev, 1)
            dve.tensor_copy(affT[:, N_LAT:], ps[6][0:EXPERTS, 0:N_CTX]).then_inc(aff_ev, 1)
            n = 0
            rounds = [(0, N_LAT, 8 * r, 2) for r in range(CAP_LAT // 8)] + [(N_LAT, N_TOK, CAP_LAT + 8 * r, 2) for r in range(CAP_CTX // 8)]
            dve.wait_ge(aff_ev, 2)
            for a, b, s0, _ in rounds:
                v8 = val[:, s0:s0 + 8]
                dve.max(v8, affT[:, a:b]).then_inc(picked, 1)
                n += 1
                dve.wait_ge(picked, n)
                dve.max_index(idx[:, s0:s0 + 8], v8, affT[:, a:b]).then_inc(picked, 1)
                dve.match_replace(affT[:, a:b], v8, affT[:, a:b], -1.0).then_inc(picked, 1)
                n += 2
                dve.wait_ge(picked, n)
            dve.tensor_copy(idx_f[:], idx[:]).then_inc(picked, 1)
            dve.wait_ge(picked, n + 1)
            dve.tensor_scalar(idx_f[:, 0:CAP_LAT], idx_f[:, 0:CAP_LAT], float(N_CTX), None, ALU.add).then_inc(picks, 1)
            dve.wait_ge(pick_tr, 1)
            dve.tensor_copy(M.gates[:], ps[7][0:SLOTS, 0:EXPERTS]).then_inc(pick_ok, 1)
            dve.tensor_copy(M.rows[:], ps[7][0:SLOTS, EXPERTS:2 * EXPERTS]).then_inc(pick_ok, 1)
            dve.wait_ge(pick_ok, 2)

        @block.tensor
        def _(pe):
            pe.wait_ge(w_in, 16)

            def route(t):
                pe.wait_ge(h_ev, 4 * t + 4)
                for k in range(KT):
                    ins = pe.matmul(ps[4][:, bass.ts(t, EXPERTS)], hT[t % 2][:, k, :], w_r[:, k, :], start=(k == 0), stop=(k == KT - 1))
                ins.then_inc(logit, 1)

            for t in range(TT):
                pe.wait_ge(h_ok, t + 1)
                for q in range(4):
                    if t:
                        pe.wait_ge(h_ev, 4 * (t - 1) + q + 1)
                    for j in range(4):
                        ins = pe.transpose(ps[q][:, bass.ts(j, P)], xr[t % 2][:, bass.ts(4 * q + j, P)], M.ident[:])
                    ins.then_inc(h_tr, 1)
                if t:
                    route(t - 1)
            route(TT - 1)
            for t in range(TT):
                pe.wait_ge(aff_ok, t + 1)
                out = ps[6][0:EXPERTS, 0:P] if t == 0 else ps[5][0:EXPERTS, bass.ts(t - 1, P)]
                pe.transpose(out, aff[:, t, :], M.ident[:]).then_inc(aff_tr, 1)
            pe.wait_ge(picks, 1)
            pe.transpose(ps[7][0:SLOTS, 0:EXPERTS], val[:], M.ident[0:EXPERTS, 0:EXPERTS])
            pe.transpose(ps[7][0:SLOTS, EXPERTS:2 * EXPERTS], idx_f[:], M.ident[0:EXPERTS, 0:EXPERTS]).then_inc(pick_tr, 1)


def phase_experts(nc, M, I, W):
    m = Map(nc, M.route_at)
    xg = m.new("xg", [SLOTS, D], F32)
    xT_hi, xT_lo = (m.new(f"xgT_{h}", [P, KT, SLOTS], F32R) for h in ("hi", "lo"))
    sil = m.new("silu_a", [SLOTS, D_FF], F32)
    hid = m.new("hidden", [SLOTS, D_FF], F32)
    HK = D_FF // P
    hT_hi, hT_lo = (m.new(f"hiddenT_{h}", [P, HK, SLOTS], F32R) for h in ("hi", "lo"))
    y = m.new("expert_y", [SLOTS, D], F32)
    cur_g = m.new("rows_gather", [SLOTS, 1], U32)
    cur_s = m.new("rows_scatter", [SLOTS, 1], U32)
    cur_gate = m.new("gate_now", [SLOTS, 1], F32)
    PB, NP = 8, 24
    N0 = 2 * PB
    LEAD, NS, NW = 3, 4, 3
    TXG = ((0, 6), (6, 12), (12, 16))

    with ExitStack() as ctx:
        sem = phase_semaphores(ctx, nc)
        pair = [ctx.enter_context(nc.psum_tensor(f"e_ps{b}", [P, 2, NC], F32)) for b in range(4)]
        s = Stream(sem, "ew", NS, NW)
        gathered, scattered = M.pool_sem("gathered"), M.pool_sem("scattered")
        idx_g, idx_s, passed, y_free = sem("idx_g"), sem("idx_s"), sem("e_passed"), sem("y_free")
        x_tr, x_hi, x_lo, sil_ok, hid_ok, h_tr, h_hi, h_lo, y_done, y_ev = (
            sem(f"e_{n}") for n in ("x_tr", "x_hi", "x_lo", "sil_ok", "hid_ok", "h_tr", "h_hi", "h_lo", "y_done", "y_ev"))
        block = ctx.enter_context(nc.Block())
        E13 = [I[n][0].rearrange("e (q j p) n -> e q p j n", j=2, p=P) for n in ("w_e1", "w_e3")]
        E2 = I["w_e2"][0].rearrange("e (q j p) (c n) -> e c q p j n", j=2, p=P, c=2)

        @block.sync
        def _(sp):
            def load(n, slot, src):
                load_piece(sp, s, n, slot, W.stage[:, slot, :].rearrange("p (j n) -> p j n", j=2), src)

            def first(e, n, j0):
                for which in range(2):
                    for q in range(PB):
                        load(n + PB * which + q, q % NS, E13[which][e, q])

            def last(e, n):
                for c in range(2):
                    for q in range(PB // 2):
                        load(n + 4 * c + q, q % NS, E2[e, c, q])

            first(0, 0, 0)
            with sp.Fori(0, EXPERTS - 1) as i:
                first(i + 1, NP * i + N0, 0)
                last(i, NP * i + N0 + 2 * PB)
            last(EXPERTS - 1, NP * (EXPERTS - 1) + N0)

        @block.gpsimd
        def _(pool):
            pool.sem_inc(y_free, 1)
            pool.sem_inc(x_tr, 3)

            def gather(e):
                pool_wait(pool, x_tr, 3 * e + 3, passed)
                pool.tensor_copy(cur_g[:], M.rows[:, bass.ds(e, 1)]).then_inc(idx_g, 1)
                pool_wait(pool, idx_g, e + 1, passed)
                pool.indirect_dma_start(out=xg[:], out_offset=None, in_=M.h2,
                                        in_offset=bass.IndirectOffsetOnAxis(ap=cur_g[:, 0:1], axis=0)).then_inc(gathered, 16)

            def scatter(e):
                pool.tensor_copy(cur_s[:], M.rows[:, bass.ds(e, 1)]).then_inc(idx_s, 1)
                pool.tensor_copy(cur_gate[:], M.gates[:, bass.ds(e, 1)]).then_inc(idx_s, 1)
                pool_wait(pool, idx_s, 2 * e + 2, passed)
                pool_wait(pool, y_ev, 2 * e + 3, passed)
                pool.indirect_dma_start(out=M.moe, out_offset=bass.IndirectOffsetOnAxis(ap=cur_s[:, 0:1], axis=0),
                                        in_=y[:], in_offset=None, compute_op=ALU.add).then_inc(scattered, 16)
                pool_wait(pool, scattered, 16 * e + 16, y_free)

            gather(0)
            gather(1)
            with pool.Fori(0, EXPERTS - 2) as i:
                gather(i + 2)
                scatter(i)
            scatter(EXPERTS - 2)
            scatter(EXPERTS - 1)

        def turned_rows(e, g, hi):
            a, b = TXG[g]
            return (xT_hi if hi else xT_lo)[:, a:b, :], pair[3][:, g % 2, 0:(b - a) * SLOTS].rearrange("p (k n) -> p k n", n=SLOTS)

        @block.scalar
        def _(act):
            def hi(n, j, i):
                slot = j % NS
                uses = j // NS + 1 if i is None else N0 // NS + NP // NS * i + j // NS + 1
                w = j % NW if i is None else (N0 + j) % NW
                piece_hi(act, s, n, slot, uses, W.hi[:, w, :], W.stage[:, slot, :])

            def rows_hi(e, g):
                act.wait_ge(x_tr, 3 * e + g + 4)
                dst, src = turned_rows(e, g, True)
                act.activation(dst, src, ACT.Copy).then_inc(x_hi, 1)

            def silu(e):
                act.wait_ge(s.used, NW + PB if isinstance(e, int) and e == 0 else NW + N0 + NP * (e - 1) + PB)
                act.activation(sil[:].rearrange("p (c n) -> p c n", c=2), pair[0][0:SLOTS, :, :], ACT.Silu).then_inc(sil_ok, 1)

            def hidden_hi(e):
                act.wait_ge(h_tr, e + 1)
                act.activation(hT_hi[:].rearrange("p (c k) n -> p c k n", c=2), pair[3][:, :, 0:HK // 2 * SLOTS].rearrange("p c (k n) -> p c k n", n=SLOTS),
                               ACT.Copy).then_inc(h_hi, 1)

            def out(e, c):
                act.wait_ge(y_done, 2 * e + c + 1)
                if c == 0:
                    act.wait_ge(y_free, e + 1)
                    act.wait_ge(idx_s, 2 * e + 2)
                act.activation(y[:, bass.ts(c, D // 2)].rearrange("p (c n) -> p c n", c=2), pair[2][0:SLOTS, :, :], ACT.Copy,
                               scale=cur_gate[:]).then_inc(y_ev, 1)

            def body(i, rows=True):
                n0 = NP * i + N0
                for j in range(NP):
                    hi(n0 + j + LEAD, j + LEAD, i)
                    if j == 7:
                        silu(i + 1)
                    if j == 8:
                        hidden_hi(i)
                    if j == 16 and rows:
                        rows_hi(i + 2, 0)
                        rows_hi(i + 2, 1)
                    if j == 19:
                        out(i, 0)
                    if j == 20 and rows:
                        rows_hi(i + 2, 2)
                    if j == 23:
                        out(i, 1)

            for g in range(3):
                rows_hi(0, g)
            for j in range(LEAD):
                hi(j, j, None)
            for j in range(N0):
                hi(j + LEAD, j + LEAD, None)
                if j == 7:
                    silu(0)
            for g in range(3):
                rows_hi(1, g)
            with act.Fori(0, EXPERTS - 2) as i:
                body(i)
            body(EXPERTS - 2, rows=False)
            n0 = NP * (EXPERTS - 1) + N0
            hidden_hi(EXPERTS - 1)
            for j in range(PB):
                if j + LEAD < PB:
                    hi(n0 + j + LEAD, j + LEAD, EXPERTS - 1)
                if j == 3:
                    out(EXPERTS - 1, 0)
                if j == 7:
                    out(EXPERTS - 1, 1)

        @block.vector
        def _(dve):
            dve.sem_inc(s.split, NS)
            sub = lambda out, src, part: dve.tensor_tensor(out, src, part.bitcast(F32), ALU.subtract)

            def lo(n, j, i):
                slot = j % NS
                w = j % NW if i is None else (N0 + j) % NW
                piece_lo(dve, s, n, W.lo[:, w, :], W.stage[:, slot, :], W.hi[:, w, :])

            def rows_lo(e, g):
                dve.wait_ge(x_hi, 3 * e + g + 1)
                dst, src = turned_rows(e, g, False)
                sub(dst, src, turned_rows(e, g, True)[0]).then_inc(x_lo, 1)

            def hidden(e):
                dve.wait_ge(s.used, NW + N0 if isinstance(e, int) and e == 0 else NW + N0 + NP * (e - 1) + 2 * PB)
                dve.wait_ge(sil_ok, e + 1)
                dve.tensor_tensor(hid[:].rearrange("p (c n) -> p c n", c=2), pair[1][0:SLOTS, :, :],
                                  sil[:].rearrange("p (c n) -> p c n", c=2), ALU.mult).then_inc(hid_ok, 1)

            def hidden_lo(e):
                dve.wait_ge(h_hi, e + 1)
                sub(hT_lo[:].rearrange("p (c k) n -> p c k n", c=2), pair[3][:, :, 0:HK // 2 * SLOTS].rearrange("p c (k n) -> p c k n", n=SLOTS),
                    hT_hi[:].rearrange("p (c k) n -> p c k n", c=2)).then_inc(h_lo, 1)

            def body(i, rows=True):
                n0 = NP * i + N0
                for j in range(NP):
                    lo(n0 + j + LEAD, j + LEAD, i)
                    if j == 8:
                        hidden_lo(i)
                    if j == 15:
                        hidden(i + 1)
                    if j == 16 and rows:
                        rows_lo(i + 2, 0)
                        rows_lo(i + 2, 1)
                    if j == 20 and rows:
                        rows_lo(i + 2, 2)

            for g in range(3):
                rows_lo(0, g)
            for j in range(LEAD):
                lo(j, j, None)
            for j in range(N0):
                lo(j + LEAD, j + LEAD, None)
            hidden(0)
            for g in range(3):
                rows_lo(1, g)
            with dve.Fori(0, EXPERTS - 2) as i:
                body(i)
            body(EXPERTS - 2, rows=False)
            n0 = NP * (EXPERTS - 1) + N0
            hidden_lo(EXPERTS - 1)
            for j in range(PB):
                if j + LEAD < PB:
                    lo(n0 + j + LEAD, j + LEAD, EXPERTS - 1)

        @block.tensor
        def _(pe):
            pe.sem_inc(s.used, NW)
            pe.sem_inc(y_ev, 1)

            def turn_rows(e, g):
                if g == 0:
                    pe.wait_ge(gathered, 16 * e + 16)
                if g == 2:
                    pe.wait_ge(x_lo, 3 * e + 1)
                a, b = TXG[g]
                for k in range(a, b):
                    ins = pe.transpose(pair[3][:, g % 2, bass.ts(k - a, SLOTS)], xg[:, bass.ts(k, P)], M.ident[0:SLOTS, 0:SLOTS])
                ins.then_inc(x_tr, 1)

            def up(n, q, w, out):
                pe.wait_ge(s.split, n + 1 + NS)
                for j in range(2):
                    k = 2 * q + j
                    for c in range(2):
                        cols = slice(j * D_FF + c * NC, j * D_FF + (c + 1) * NC)
                        ins = product(pe, out[0:SLOTS, c, :], xT_hi[:, k, :], xT_lo[:, k, :], W.hi[:, w, cols], W.lo[:, w, cols], k == 0, k == KT - 1)
                ins.then_inc(s.used, 1)

            def turn_hidden(e):
                pe.wait_ge(hid_ok, e + 1)
                for k in range(HK):
                    ins = pe.transpose(pair[3][:, k // (HK // 2), bass.ts(k % (HK // 2), SLOTS)], hid[:, bass.ts(k, P)], M.ident[0:SLOTS, 0:SLOTS])
                ins.then_inc(h_tr, 1)

            def down(e, n, c, q, w):
                if q == 0:
                    pe.wait_ge(y_ev, 2 * e + c + 1)
                    if c == 0:
                        pe.wait_ge(h_lo, e + 1)
                pe.wait_ge(s.split, n + 1 + NS)
                for j in range(2):
                    k = 2 * q + j
                    for cc in range(2):
                        cols = slice(j * D // 2 + cc * NC, j * D // 2 + (cc + 1) * NC)
                        ins = product(pe, pair[2][0:SLOTS, cc, :], hT_hi[:, k, :], hT_lo[:, k, :], W.hi[:, w, cols], W.lo[:, w, cols], k == 0, k == HK - 1)
                ins.then_inc(s.used, 1)
                if q == PB // 2 - 1:
                    pe.wait_ge(s.used, n + 1 + NW)
                    pe.sem_inc(y_done, 1)

            def body(i, rows=True):
                n0 = NP * i + N0
                pe.wait_ge(x_lo, 3 * i + 6)
                pe.wait_ge(sil_ok, i + 1)
                for q in range(PB):
                    up(n0 + q, q, (N0 + q) % NW, pair[0])
                turn_hidden(i)
                for q in range(PB):
                    up(n0 + PB + q, q, (N0 + PB + q) % NW, pair[1])
                for c in range(2):
                    for q in range(PB // 2):
                        j = 2 * PB + 4 * c + q
                        down(i, n0 + j, c, q, (N0 + j) % NW)
                        if j == 16 and rows:
                            turn_rows(i + 2, 0)
                            turn_rows(i + 2, 1)
                        if j == 20 and rows:
                            turn_rows(i + 2, 2)

            for g in range(3):
                turn_rows(0, g)
            pe.wait_ge(x_lo, 3)
            for q in range(PB):
                up(q, q, q % NW, pair[0])
            for q in range(PB):
                up(PB + q, q, (PB + q) % NW, pair[1])
            for g in range(3):
                turn_rows(1, g)
            with pe.Fori(0, EXPERTS - 2) as i:
                body(i)
            body(EXPERTS - 2, rows=False)
            n0 = NP * (EXPERTS - 1) + N0
            turn_hidden(EXPERTS - 1)
            for c in range(2):
                for q in range(PB // 2):
                    down(EXPERTS - 1, n0 + 4 * c + q, c, q, (N0 + 4 * c + q) % NW)


def phase_final(nc, M, I, W, O):
    m = Map(nc, M.phase_at)
    xr = [m.new(f"f_x{b}", [P, D], F32) for b in range(2)]
    moe = [m.new(f"f_moe{b}", [P, D], F32) for b in range(2)]
    gate = m.new("f_gate2", [P, 2, D], F32)
    g_row = m.new("f_g", [P, D], F32)
    square = m.new("f_square", [P, D], F32)
    st = m.new("f_stats", [P, 4, TT], F32)
    with ExitStack() as ctx:
        sem = phase_semaphores(ctx, nc)
        x_in, y_out = [sem("f_x_in0"), sem("f_x_in1")], [sem("f_y_out0"), sem("f_y_out1")]
        rows_in, g_in, gated, summed, sq, var, std, inv, y_ok = (
            sem(f"f_{n}") for n in ("rows_in", "g_in", "gated", "summed", "sq", "var", "std", "inv", "y_ok"))
        block = ctx.enter_context(nc.Block())

        @block.sync
        def _(sp):
            def load(t):
                if t >= 2:
                    sp.wait_ge(y_out[t % 2], 16 * (t // 2))
                sp.dma_start(xr[t % 2][:], M.xn[bass.ts(t, P), :]).then_inc(x_in[t % 2], 16)
                sp.dma_start(moe[t % 2][:], M.moe[bass.ts(t, P), :]).then_inc(x_in[t % 2], 16)
            for r in range(2):
                sp.dma_start(gate[:, r, :], M.mod[r:r + 1, 5 * D:6 * D].to_broadcast((P, D))).then_inc(rows_in, 16)
            load(0)
            sp.dma_start(g_row[:], I["g_final"].rearrange("(a n) -> a n", a=1).to_broadcast((P, D))).then_inc(g_in, 16)
            for t in range(TT):
                if t + 1 < TT:
                    load(t + 1)
                sp.wait_ge(y_ok, t + 1)
                dst = O["y_prompt"][0] if t == 0 else O["y_sample"][0, bass.ts(t - 1, P), :]
                sp.dma_start(dst, xr[t % 2][:]).then_inc(y_out[t % 2], 16)
            sp.wait_ge(y_out[0], 16 * ((TT + 1) // 2))
            sp.wait_ge(y_out[1], 16 * (TT // 2))

        @block.scalar
        def _(act):
            for t in range(TT):
                act.wait_ge(summed, t + 1)
                if t:
                    act.wait_ge(sq, t)
                act.activation(square[:], xr[t % 2][:], ACT.Square, accum_out=st[:, 0, t:t + 1]).then_inc(sq, 1)
                act.wait_ge(var, t + 1)
                act.activation(st[:, 2, t:t + 1], st[:, 1, t:t + 1], ACT.Sqrt).then_inc(std, 1)

        @block.vector
        def _(dve):
            def add(t):
                dve.wait_ge(x_in[t % 2], 32 * (t // 2 + 1))
                dve.tensor_tensor(moe[t % 2][:], moe[t % 2][:], gate[:, min(t, 1), :], ALU.mult).then_inc(gated, 1)
                dve.wait_ge(gated, t + 1)
                dve.tensor_tensor(xr[t % 2][:], xr[t % 2][:], moe[t % 2][:], ALU.add).then_inc(summed, 1)
            dve.wait_ge(rows_in, 32)
            add(0)
            dve.wait_ge(g_in, 16)
            for t in range(TT):
                if t + 1 < TT:
                    add(t + 1)
                dve.wait_ge(sq, t + 1)
                dve.tensor_scalar(st[:, 1, t:t + 1], st[:, 0, t:t + 1], 1.0 / D, EPS, ALU.mult, ALU.add).then_inc(var, 1)
                dve.wait_ge(std, t + 1)
                dve.reciprocal(st[:, 3, t:t + 1], st[:, 2, t:t + 1]).then_inc(inv, 1)
                dve.wait_ge(inv, t + 1)
                dve.scalar_tensor_tensor(xr[t % 2][:], xr[t % 2][:], st[:, 3, t:t + 1], g_row[:], ALU.mult, ALU.mult).then_inc(y_ok, 1)


def rope_angles():
    t = np.arange(N_LAT)
    inv = 1.0 / (10000.0 ** (np.arange(ROPE_FREQS, dtype=np.float32) / ROPE_FREQS))
    inv = inv.astype(np.float32)
    return np.stack([(t // 64).astype(np.float32)[:, None] * inv, (t % 64).astype(np.float32)[:, None] * inv], 1)


def constants():
    a = rope_angles()
    cos = np.ones((N_TOK, 2, 2, ROPE_FREQS), np.float32)
    sin = np.zeros((N_TOK, 2, 2, ROPE_FREQS), np.float32)
    cos[N_CTX:] = np.cos(a)[:, :, None, :]
    sin[N_CTX:] = np.stack([-np.sin(a), np.sin(a)], 2)
    rows = np.concatenate([cos.reshape(N_TOK, D_ROPE), sin.reshape(N_TOK, D_ROPE)], 1)
    return {"rope_rows": rows, "rope_cols": np.ascontiguousarray(rows.T)}


def build(nc, I, O, phases=99):
    outer = ExitStack()
    M, W = Names(), Names()
    M.pool_sem = lambda name: outer.enter_context(nc.semaphore(name))
    keep = Map(nc, SBUF_FROM)
    M.ident = keep.new("ident", [P, P], F32)
    M.c_st = keep.new("c_st", [P, KT, 34], F32R)
    W.at = keep.at
    W.stage = keep.new("w_stage", [P, 4, PIECE], F32)
    W.hi = keep.new("w_hi", [P, 3, PIECE], F32R)
    W.spare_at = keep.at - 4 * PIECE
    W.lo = keep.new("w_lo", [P, 3, PIECE], F32R)
    M.phase_at = keep.at
    dram = lambda name, shape: nc.dram_tensor(name, shape, F32, kind="Internal").ap()
    M.mod = dram("mod", [2, 6 * D])
    M.acts = dram("acts", [N_TOK, 4 * D])
    M.oaT = dram("oaT", [D, N_TOK])
    M.ma = dram("ma", [N_TOK, D])
    M.mT = dram("mT", [D, N_TOK])
    M.xn = dram("xn", [N_TOK, D])
    M.h2 = dram("h2", [N_TOK, D])
    M.moe = dram("moe", [N_TOK, D])
    M.obT = dram("obT", [D, N_TOK])
    todo = [lambda: phase_modulate(nc, M, I, W), lambda: phase_in_proj(nc, M, I, W), lambda: phase_mix(nc, M, I, W, O),
            lambda: phase_heads(nc, M, I, W),
            *((lambda kind=kind: phase_project(nc, M, I, W, kind)) for kind in ("mla", "gm", "out")),
            lambda: phase_route(nc, M, I, W), lambda: phase_experts(nc, M, I, W), lambda: phase_final(nc, M, I, W, O)]
    for phase in todo[:phases]:
        phase()
    outer.close()


_OUTS = {"y_prompt": (1, N_CTX, D), "y_sample": (1, N_LAT, D), "new_ckv": (1, 1, N_CTX, KV_LORA), "new_krope": (1, 1, N_CTX, D_ROPE)}


def kernel(**inputs):
    import concourse.bacc as bacc
    from concourse.bass_utils import run_bass_kernel_spmd

    nc = bacc.Bacc("TRN2", target_bir_lowering=False, num_devices=1)
    arrays, I, O = {}, {}, {}
    for name, a in {**inputs, **constants()}.items():
        a = np.ascontiguousarray(a)
        arrays[f"in_{name}"] = a
        I[name] = nc.dram_tensor(f"in_{name}", a.shape, mybir.dt.from_np(a.dtype), kind="ExternalInput").ap()
    for name, shape in _OUTS.items():
        O[name] = nc.dram_tensor(f"out_{name}", shape, F32, kind="ExternalOutput").ap()
    build(nc, I, O)
    r = run_bass_kernel_spmd(nc, [arrays], core_ids=[0])
    return tuple(r.results[0][f"out_{name}"] for name in _OUTS)
```
